# Optimizing a Trainium2 kernel written in Bass

```python
import math
import jax
import jax.numpy as jnp
from jax import lax
import numpy as np

D_MODEL = 2048
BATCH = 1
SEQ = 256
DEPTH = 2

N_MIXERS = 2
N_MLA = (DEPTH + N_MIXERS - 1) // N_MIXERS
N_HGRN = DEPTH // N_MIXERS
RMS_EPS = 1e-6

MLA_HEADS = 16
Q_LORA = 512
KV_LORA = 512
QK_NOPE = 128
QK_ROPE = 64
QK_HEAD = QK_NOPE + QK_ROPE
V_HEAD = 128
MLA_A_DIM = Q_LORA + KV_LORA + QK_ROPE
ROPE_THETA = 10000.0
Q_BLOCK = 128

HGRN_HEADS = 16
HGRN_EXPAND = 128
HGRN_HEAD_V = D_MODEL // HGRN_HEADS
HGRN_FDIM = HGRN_HEADS * HGRN_EXPAND
HGRN_VDIM = HGRN_HEADS * HGRN_HEAD_V
HGRN_IN_DIM = 2 * HGRN_FDIM + 2 * HGRN_VDIM
CHUNK = 64

D_FF = 5632
CONV_W = 3

PLE_DIM = 256

kernel_name = 'hybrid_mla_hgrn2_convffn_ple'

def rms_norm(x, g):
    xf = x.astype(jnp.float32)
    y = xf * lax.rsqrt(jnp.mean(xf * xf, axis=-1, keepdims=True) + RMS_EPS)
    return (y * g.astype(jnp.float32)).astype(x.dtype)

def rope_tables(positions):
    inv_freq = ROPE_THETA ** (-jnp.arange(0, QK_ROPE, 2, dtype=jnp.float32) / QK_ROPE)
    ang = positions.astype(jnp.float32)[..., None] * inv_freq
    return jnp.cos(ang), jnp.sin(ang)

def apply_rope(x, cos, sin):
    c = cos[:, :, None, :].astype(x.dtype)
    s = sin[:, :, None, :].astype(x.dtype)
    x1, x2 = jnp.split(x, 2, axis=-1)
    return jnp.concatenate([x1 * c - x2 * s, x2 * c + x1 * s], axis=-1)

def causal_block_attention(q, k, v):
    B, S, H, dq = q.shape
    dv = v.shape[-1]
    nb = S // Q_BLOCK
    scale = 1.0 / math.sqrt(dq)
    kt = k.transpose(0, 2, 1, 3)
    vt = v.transpose(0, 2, 1, 3)
    qb = q.reshape(B, nb, Q_BLOCK, H, dq).transpose(1, 0, 3, 2, 4)
    key_pos = jnp.arange(S)

    def one_block(args):
        qblk, bi = args
        s = jnp.einsum('bhqd,bhkd->bhqk', qblk, kt).astype(jnp.float32) * scale
        q_pos = bi * Q_BLOCK + jnp.arange(Q_BLOCK)
        mask = key_pos[None, :] <= q_pos[:, None]
        s = jnp.where(mask, s, -jnp.inf)
        pr = jax.nn.softmax(s, axis=-1).astype(vt.dtype)
        return jnp.einsum('bhqk,bhkd->bhqd', pr, vt)

    o = lax.map(one_block, (qb, jnp.arange(nb)))
    return o.transpose(1, 0, 3, 2, 4).reshape(B, S, H * dv)

def mla_mixer(xn, cos, sin, w_a, q_norm, w_uq, kv_norm, w_ukv, qk_gain_q, qk_gain_k, w_o):
    B, S, _ = xn.shape
    c = xn @ w_a
    c_q = c[..., :Q_LORA]
    c_kv = c[..., Q_LORA:Q_LORA + KV_LORA]
    k_pe = c[..., Q_LORA + KV_LORA:]
    q = (rms_norm(c_q, q_norm) @ w_uq).reshape(B, S, MLA_HEADS, QK_HEAD)
    kv = (rms_norm(c_kv, kv_norm) @ w_ukv).reshape(B, S, MLA_HEADS, QK_NOPE + V_HEAD)
    k_nope = kv[..., :QK_NOPE]
    v = kv[..., QK_NOPE:]
    k = jnp.concatenate([k_nope, jnp.broadcast_to(k_pe[:, :, None, :], (B, S, MLA_HEADS, QK_ROPE))], axis=-1)
    q = rms_norm(q, qk_gain_q)
    k = rms_norm(k, qk_gain_k)
    q = jnp.concatenate([q[..., :QK_NOPE], apply_rope(q[..., QK_NOPE:], cos, sin)], axis=-1)
    k = jnp.concatenate([k[..., :QK_NOPE], apply_rope(k[..., QK_NOPE:], cos, sin)], axis=-1)
    o = causal_block_attention(q, k, v)
    return o @ w_o

def _hgrn_chunk_step(state, inp):
    q, k, v, log_f = inp
    b = jnp.cumsum(log_f, axis=2)
    o_inter = jnp.einsum('bhtd,bhde->bhte', q * jnp.exp(b), state)
    diff = b[:, :, :, None, :] - b[:, :, None, :, :]
    causal = jnp.tril(jnp.ones((CHUNK, CHUNK), dtype=bool))
    decay = jnp.exp(jnp.where(causal[:, :, None], diff, -jnp.inf))
    a = jnp.einsum('bhtd,bhsd,bhtsd->bhts', q, k, decay)
    o = o_inter + jnp.einsum('bhts,bhse->bhte', a, v)
    b_last = b[:, :, -1:, :]
    new_state = jnp.exp(b_last[:, :, 0, :])[..., None] * state + jnp.einsum('bhsd,bhse->bhde', k * jnp.exp(b_last - b), v)
    return new_state, o

def hgrn2_mixer(xn, lb, w_in, o_norm, w_o):
    B, T, _ = xn.shape
    nc = T // CHUNK
    f32 = jnp.float32
    z = xn @ w_in
    q_raw = z[..., :HGRN_FDIM]
    f_raw = z[..., HGRN_FDIM:2 * HGRN_FDIM]
    i_in = z[..., 2 * HGRN_FDIM:2 * HGRN_FDIM + HGRN_VDIM]
    g = z[..., 2 * HGRN_FDIM + HGRN_VDIM:]
    lbf = lb.astype(f32)
    ff = f_raw.astype(f32)
    log_f = jnp.log(lbf + (1.0 - lbf) * jax.nn.sigmoid(ff))
    k = (1.0 - lbf) * jax.nn.sigmoid(-ff)
    q = jax.nn.silu(q_raw.astype(f32))
    v = i_in.astype(f32)

    def to_chunks(t, d):
        return t.reshape(B, nc, CHUNK, HGRN_HEADS, d).transpose(1, 0, 3, 2, 4)

    s0 = jnp.zeros((B, HGRN_HEADS, HGRN_EXPAND, HGRN_HEAD_V), f32)
    _, o = lax.scan(_hgrn_chunk_step, s0, (to_chunks(q, HGRN_EXPAND), to_chunks(k, HGRN_EXPAND), to_chunks(v, HGRN_HEAD_V), to_chunks(log_f, HGRN_EXPAND)))
    o = o.transpose(1, 0, 3, 2, 4).reshape(B, T, HGRN_HEADS, HGRN_HEAD_V)
    o = rms_norm(o, o_norm.reshape(HGRN_HEADS, HGRN_HEAD_V)).astype(xn.dtype).reshape(B, T, HGRN_VDIM)
    o = o * jax.nn.silu(g)
    return o @ w_o

def conv_ffn(xn, w_in, conv_w, conv_b, w_down):
    T = xn.shape[1]
    gu = xn @ w_in
    gate = gu[..., :D_FF]
    up = gu[..., D_FF:]
    gp = jnp.pad(gate, ((0, 0), (CONV_W - 1, 0), (0, 0)))
    conv = conv_b + gp[:, 0:T] * conv_w[0]
    for tap in range(1, CONV_W):
        conv = conv + gp[:, tap:tap + T] * conv_w[tap]
    return (jax.nn.silu(conv) * up) @ w_down

def per_layer_embedding(h, p_i, norm_g, w_proj, w_gate):
    return (p_i @ w_proj) * jax.nn.sigmoid(rms_norm(h, norm_g) @ w_gate)

def _w(k, shape, fan_in):
    return jax.random.normal(k, shape, jnp.float32) * (fan_in ** -0.5)

def _gain(k, shape):
    return 1.0 + 0.02 * jax.random.normal(k, shape, jnp.float32)

def setup_inputs(seed: int = 0) -> dict:
    key = jax.random.key(seed)
    ks = jax.random.split(key, 26)
    x = jax.random.normal(ks[0], (BATCH, SEQ, D_MODEL), jnp.float32)
    p = jax.random.normal(ks[1], (DEPTH, BATCH, SEQ, PLE_DIM), jnp.float32)
    positions = (jnp.arange(SEQ, dtype=jnp.int32)[None, :] + jax.random.randint(ks[2], (BATCH, 1), 0, 4096, dtype=jnp.int32)).astype(jnp.int32)
    return {
        'x': x,
        'p': p,
        'positions': positions,
        'mix_norm': _gain(ks[3], (DEPTH, D_MODEL)),
        'ffn_norm': _gain(ks[4], (DEPTH, D_MODEL)),
        'ple_norm': _gain(ks[5], (DEPTH, D_MODEL)),
        'mla_w_a': _w(ks[6], (N_MLA, D_MODEL, MLA_A_DIM), D_MODEL),
        'mla_q_norm': _gain(ks[7], (N_MLA, Q_LORA)),
        'mla_w_uq': _w(ks[8], (N_MLA, Q_LORA, MLA_HEADS * QK_HEAD), Q_LORA),
        'mla_kv_norm': _gain(ks[9], (N_MLA, KV_LORA)),
        'mla_w_ukv': _w(ks[10], (N_MLA, KV_LORA, MLA_HEADS * (QK_NOPE + V_HEAD)), KV_LORA),
        'mla_qk_gain_q': _gain(ks[11], (N_MLA, QK_HEAD)),
        'mla_qk_gain_k': _gain(ks[12], (N_MLA, QK_HEAD)),
        'mla_w_o': _w(ks[13], (N_MLA, MLA_HEADS * V_HEAD, D_MODEL), MLA_HEADS * V_HEAD),
        'hgrn_lb_logits': 0.5 * jax.random.normal(ks[14], (DEPTH, HGRN_FDIM), jnp.float32),
        'hgrn_w_in': _w(ks[15], (N_HGRN, D_MODEL, HGRN_IN_DIM), D_MODEL),
        'hgrn_o_norm': _gain(ks[16], (N_HGRN, HGRN_VDIM)),
        'hgrn_w_o': _w(ks[17], (N_HGRN, HGRN_VDIM, D_MODEL), HGRN_VDIM),
        'ffn_w_in': _w(ks[18], (DEPTH, D_MODEL, 2 * D_FF), D_MODEL),
        'ffn_conv_w': _w(ks[19], (DEPTH, CONV_W, D_FF), CONV_W),
        'ffn_conv_b': 0.01 * jax.random.normal(ks[20], (DEPTH, D_FF), jnp.float32),
        'ffn_w_down': _w(ks[21], (DEPTH, D_FF, D_MODEL), D_FF),
        'ple_w_proj': _w(ks[22], (DEPTH, PLE_DIM, D_MODEL), PLE_DIM),
        'ple_w_gate': _w(ks[23], (DEPTH, D_MODEL, D_MODEL), D_MODEL),
    }

def reference(x, p, positions, mix_norm, ffn_norm, ple_norm, mla_w_a, mla_q_norm, mla_w_uq, mla_kv_norm, mla_w_ukv, mla_qk_gain_q, mla_qk_gain_k, mla_w_o, hgrn_lb_logits, hgrn_w_in, hgrn_o_norm, hgrn_w_o, ffn_w_in, ffn_conv_w, ffn_conv_b, ffn_w_down, ple_w_proj, ple_w_gate):
    cos, sin = rope_tables(positions)
    sm = jax.nn.softmax(hgrn_lb_logits.astype(jnp.float32), axis=0)
    lower_bounds = jnp.cumsum(sm, axis=0) - sm[0]
    h = x
    for i in range(DEPTH):
        j = i // N_MIXERS
        xn = rms_norm(h, mix_norm[i])
        if i % N_MIXERS == 0:
            h = h + mla_mixer(xn, cos, sin, mla_w_a[j], mla_q_norm[j], mla_w_uq[j], mla_kv_norm[j], mla_w_ukv[j], mla_qk_gain_q[j], mla_qk_gain_k[j], mla_w_o[j])
        else:
            h = h + hgrn2_mixer(xn, lower_bounds[i], hgrn_w_in[j], hgrn_o_norm[j], hgrn_w_o[j])
        h = h + conv_ffn(rms_norm(h, ffn_norm[i]), ffn_w_in[i], ffn_conv_w[i], ffn_conv_b[i], ffn_w_down[i])
        h = h + per_layer_embedding(h, p[i], ple_norm[i], ple_w_proj[i], ple_w_gate[i])
    return h


_drawn_inputs = setup_inputs


def setup_inputs(seed=0):
    import zlib

    import numpy as np

    out = dict(_drawn_inputs(seed))
    spreads = {}
    factors = {'mix_norm': 3.883,
     'ffn_norm': 3.09,
     'ple_norm': 8.0,
     'mla_q_norm': 8.0,
     'mla_kv_norm': 8.0,
     'mla_qk_gain_q': 8.0,
     'mla_qk_gain_k': 8.0,
     'hgrn_o_norm': 6.796,
     'ffn_conv_b': 8.0}
    for name, (base, spread) in spreads.items():
        noise = np.random.default_rng([zlib.crc32(name.encode()), seed]).standard_normal(out[name].shape)
        drawn = base * np.exp(spread * noise) if base else spread * noise
        out[name] = jnp.asarray(drawn.astype(out[name].dtype))
    for name, factor in factors.items():
        out[name] = (out[name] * factor).astype(out[name].dtype)
    return out
```

```python
from contextlib import ExitStack

import numpy as np

import concourse.bass as bass
from concourse import mybir

F32 = mybir.dt.float32
F32R = mybir.dt.float32r
I32 = mybir.dt.int32
ALU = mybir.AluOpType
ACT = mybir.ActivationFunctionType
AX = mybir.AxisListType

P = 128
T = 256
D = 2048
KT = D // P
HEADS = 16
PAIRS = HEADS // 2
LORA_T = 4
ROPE = 64
QK = 192
FF = 5632
FFT = FF // P
CH = 4
NCH = FFT // CH
UNIT = 16 * P
EPS = 1e-6
LEVELS = 7
GROUPS = ((0, 3), (3, 6), (6, 8))
LEAD = 3
NEG = -1.0e30

U_A = 9
U_Q, U_K, U_V = 6, 4, 4
U_O = 16
U_F = 3 * FFT
U_PP, U_PG = 2, 16
U_H = 4 * HEADS
BASE = {}
_n = 0
for _name, _c in (("a", U_A), ("q", U_Q), ("k", U_K), ("v", U_V), ("o0", U_O), ("f0", U_F), ("pp0", U_PP), ("pg0", U_PG),
                  ("h", U_H), ("o1", U_O), ("f1", U_F), ("pp1", U_PP), ("pg1", U_PG)):
    BASE[_name] = _n
    _n += _c
UNITS = _n
TILE = {}
_n = 0
for _name, _c in (("a", 9), ("q", 24), ("k", 16), ("v", 16), ("o0", 16), ("f0", 2 * FFT + 16 * NCH), ("pp0", 16), ("pg0", 16),
                  ("h", 64), ("o1", 16), ("f1", 2 * FFT + 16 * NCH), ("pp1", 16), ("pg1", 16)):
    TILE[_name] = _n
    _n += _c
H_PER_LAYER = 16 + 16 * NCH + 16

COLS = {}
_n = 0
for _name, _c in (("mix", 2 * KT), ("ffn", 2 * KT), ("ple", 2 * KT), ("cq", 4), ("ckv", 4), ("gq_nope", 1), ("gq_pe", 1),
                  ("gk_nope", 1), ("gk_pe", 1), ("o_norm", 16), ("logit0", 16), ("logit1", 16),
                  ("conv_w", 2 * 3 * FFT), ("conv_b", 2 * FFT), ("inv_freq", 1)):
    COLS[_name] = _n
    _n += _c
NCOLS = _n
ARENA_COLS = 52500


class Lin:

    def __init__(self, c, k=0, i=None):
        self.c, self.k, self.i = c, k, i

    def __add__(self, n):
        return Lin(self.c + n, self.k, self.i)

    def __sub__(self, n):
        return Lin(self.c - n, self.k, self.i)

    def __mul__(self, n):
        return Lin(self.c * n, self.k * n, self.i)

    def slot(self, m):
        assert self.k % m == 0
        return self.c % m

    def rounds(self, m):
        assert self.k % m == 0
        return Lin(self.c // m, self.k // m, self.i)

    @property
    def moving(self):
        return self.i is not None and self.k != 0

    @property
    def v(self):
        return self.i * self.k + self.c if self.moving else self.c


def count(n):
    return n.v if isinstance(n, Lin) and n.moving else max(n.c if isinstance(n, Lin) else n, 0)


AHEAD = 4
ROPE_STEPS = 27


def ahead(n):
    return count(n + AHEAD) if isinstance(n, Lin) and n.moving or count(n) else 0


def two(t, pr):
    return t[:, bass.ds((pr * 2).v, 2), :] if pr.moving else t[:, 2 * pr.c:2 * pr.c + 2, :]


def half_row(t, half, idx):
    if not idx.moving:
        return t[half, idx.c, :]
    return t[half, bass.ds(idx.v, 1), :].rearrange("p a n -> p (a n)")


class Signals:
    pass


def row(t, idx):
    if not isinstance(idx, Lin):
        idx = Lin(idx)
    if not idx.moving:
        return t[:, idx.c, :]
    return t[:, bass.ds(idx.v, 1), :].rearrange("p a n -> p (a n)")


def col(t, idx):
    return t[:, bass.ds(idx.v, 1)] if idx.moving else t[:, idx.c:idx.c + 1]


def build(nc, wstream, x_t, p_t, positions, table, mats, masks, out):
    with ExitStack() as ctx:
        cursor = [0]

        def at(name, cols, dt, offset):
            return nc.alloc_sbuf_tensor_at(name, [P] + cols, dt, offset=offset)

        ctx.enter_context(nc.sbuf_tensor("arena", [P, ARENA_COLS], F32))
        names = {}

        def sb(name, cols, dt=F32, region=None):
            size = 4 * int(np.prod(cols))
            size = (size + 31) // 32 * 32
            where = cursor if region is None else region
            t = at(name, cols, dt, ARENA + where[0])
            names[name] = (where[0], size)
            where[0] += size
            return t

        ARENA = nc.sbuf_base - ARENA_COLS * 4
        raw = sb("raw", [4, UNIT])
        whi = sb("whi", [2, UNIT], F32R)
        wlo = sb("wlo", [2, UNIT], F32R)
        h = sb("h", [KT, T])
        xa = sb("xa", [KT, 2 * T], F32R)
        rstd = sb("rstd", [T])
        sqacc = sb("sqacc", [T])
        sqb = sb("sqb", [2, T])
        lnb = sb("lnb", [T])
        p1 = sb("p1", [4, T])
        sm = sb("sm", [4, T])
        dsum = sb("dsum", [4, T])
        tab = sb("tab", [NCOLS])
        mat = sb("mat", [4, P])
        lvlmask = sb("lvlmask", [LEVELS * P + T], I32)
        lb = sb("lb", [4, HEADS])
        eps = sb("eps", [1])
        ones, ident, rot, tri = (mat[:, k, :] for k in range(4))
        zone = cursor[0]
        zb = [zone]
        xb = sb("xb", [KT, 2 * T], F32R, zb)
        z2 = zb[0]
        zm = [zone]
        c = sb("c", [9, T], F32, zm)
        xc = sb("xc", [8, 2 * T], F32R, zm)
        qn = sb("qn", [HEADS, T], F32, zm)
        qp = sb("qp", [PAIRS, T], F32, zm)
        zx = [names["xa"][0]]
        kn = sb("kn", [HEADS, T], F32, zx)
        vt = sb("vt", [2, D], F32, zx)
        cosb = sb("cosb", [T], F32, zm)
        sinb = sb("sinb", [T], F32, zm)
        kro = sb("kro", [T], F32, zm)
        skpe = sb("skpe", [T], F32, zm)
        zs = [zm[0]]
        cacc = sb("cacc", [2, T], F32, zs)
        csq = sb("csq", [2, T], F32, zs)
        cln = sb("cln", [T], F32, zs)
        rc = sb("rc", [2, T], F32, zs)
        kg = sb("kg", [T], F32, zs)
        kr = sb("kr", [2, T], F32, zs)
        top_ab = zs[0]
        zr = [names["qn"][0]]
        posi = sb("posi", [T], I32, zr)
        ang = sb("ang", [T], F32, zr)
        kk = sb("kk", [2, T], F32, zr)
        rr = sb("rr", [2, 4, T], F32, zr)
        zt = [zm[0]]
        sqq, sqp, qps, kps = sqb, sqacc, rstd, lnb
        rqk = p1[:].rearrange("p (a w) t -> p a w t", a=2)
        rq, rk = rqk[:, :, 0, :], rqk[:, :, 1, :]
        sqk = sb("sqk", [2, T], F32, zt)
        qs = sb("qs", [2, T], F32, zt)
        ks = sb("ks", [2, T], F32, zt)
        qpr = sb("qpr", [T], F32, zt)
        rt = sb("rt", [2, T], F32, zt)
        vs = sb("vs", [2, 2 * P], F32, zt)
        pts = sb("pts", [2, 3 * P], F32, zt)
        ssb = sm[:].rearrange("p (a b) t -> p a b t", a=2)
        pb = dsum[:].rearrange("p (a b) t -> p a b t", a=2)
        stat = sb("stat", [2, 4, 2], F32, zt)
        zf = [z2]
        hid = sb("hid", [2, CH, 2 * T], F32R, zf)
        gn = sb("gn", [2, T + 2], F32, zf)
        cv = sb("cv", [3, T], F32, zf)
        sl = sb("sl", [2, T], F32, zf)
        slr = sb("slr", [2, T], F32, zf)
        hv = sb("hv", [2, T], F32, zf)
        zp = [z2]
        pp = sb("pp", [KT, T], F32, zp)
        pz = sb("pz", [2, T], F32, zp)
        pg = sb("pg", [2, T], F32, zp)
        pm = sb("pm", [2, T], F32, zp)
        assert zp[0] <= zf[0]
        pt = sb("pt", [2, T], F32, zf)
        pts2 = sb("pts2", [2, 2 * T], F32R, zf)
        zh = [z2]
        fqg = sb("fqg", [3, T], F32, zh)
        sg = sb("sg", [4, T], F32, zh)
        fl = sb("fl", [T], F32, zh)
        sufpre = sb("sufpre", [2 * T], F32, zh)
        kq = sb("kq", [2 * T], F32, zh)
        gs = sb("gs", [T], F32, zh)
        vtr = sb("vtr", [T], F32, zh)
        vtok = sb("vtok", [2, P], F32, zh)
        ex = sb("ex", [2, T], F32, zh)
        cl = sb("cl", [LEVELS + 1, T], F32, zh)
        am = sb("am", [3, P], F32, zh)
        osq = sb("osq", [T], F32, zh)
        oln = sb("oln", [T], F32, zh)
        rso = sb("rso", [T], F32, zh)
        oy = sb("oy", [2, T], F32, zh)
        for top in (top_ab, zr[0], zt[0], zp[0], zh[0], zf[0]):
            assert top <= ARENA_COLS * 4, (top, ARENA_COLS * 4)

        bank = [ctx.enter_context(nc.psum_tensor(f"bank{k}", [P, 512], F32)) for k in range(8)]

        def sem(name):
            return ctx.enter_context(nc.semaphore(name))

        s = Signals()
        s.raw_in = [sem(f"raw_in{k}") for k in range(4)]
        s.x_in = [sem(f"x_in{k}") for k in range(4)]
        s.tab_in = sem("tab_in")
        s.mat_in = sem("mat_in")
        s.mask_in = sem("mask_in")
        s.pos_in = sem("pos_in")
        s.p_in = sem("p_in")
        s.out_done = sem("out_done")
        s.hi_done = sem("hi_done")
        s.lo_done = sem("lo_done")
        s.quarter_done = sem("quarter_done")
        s.p1_copied = sem("p1_copied")
        s.evacuated = sem("evacuated")
        s.x_hi = sem("x_hi")
        s.x_ready = sem("x_ready")
        s.sq_done = sem("sq_done")
        s.sq_added = sem("sq_added")
        s.norm_summed = sem("norm_summed")
        s.norm_log = sem("norm_log")
        s.rstd_ready = sem("rstd_ready")
        s.h_added = sem("h_added")
        s.gate_act = sem("gate_act")
        s.gate_pool = sem("gate_pool")
        s.gate_dve = sem("gate_dve")
        s.eps_set = sem("eps_set")
        s.lb_act = sem("lb_act")
        s.lb_dve = sem("lb_dve")
        s.pads_set = sem("pads_set")
        s.rope_step = sem("rope_step")
        s.rope_ready = sem("rope_ready")
        s.c_ready = sem("c_ready")
        s.csq_done = sem("csq_done")
        s.cacc_done = sem("cacc_done")
        s.c_summed = sem("c_summed")
        s.c_log = sem("c_log")
        s.rc_ready = sem("rc_ready")
        s.cn_ready = sem("cn_ready")
        s.xc_hi = sem("xc_hi")
        s.xc_ready = sem("xc_ready")
        s.kg_ready = sem("kg_ready")
        s.k_rotated = sem("k_rotated")
        s.k_roped = sem("k_roped")
        s.skpe_done = sem("skpe_done")
        s.v_turned = sem("v_turned")
        s.v_stored = sem("v_stored")
        s.q_squared = sem("q_squared")
        s.qk_summed = sem("qk_summed")
        s.qk_log = sem("qk_log")
        s.qk_rstd = sem("qk_rstd")
        s.qk_scaled = sem("qk_scaled")
        s.q_rotated = sem("q_rotated")
        s.q_parts = sem("q_parts")
        s.q_cos = sem("q_cos")
        s.q_roped = sem("q_roped")
        s.v_picked = sem("v_picked")
        s.scored = sem("scored")
        s.masked = sem("masked")
        s.max_step = sem("max_step")
        s.exp_done = sem("exp_done")
        s.probs_step = sem("probs_step")
        s.probs_ready = sem("probs_ready")
        s.turned = sem("turned")
        s.pt_copied = sem("pt_copied")
        s.o_done = sem("o_done")
        s.ox_hi = sem("ox_hi")
        s.ox_ready = sem("ox_ready")
        s.sq_clear = sem("sq_clear")
        s.gate_scaled = sem("gate_scaled")
        s.conv_step = sem("conv_step")
        s.conv_done = sem("conv_done")
        s.silu_done = sem("silu_done")
        s.silu_scaled = sem("silu_scaled")
        s.hid_done = sem("hid_done")
        s.hid_hi = sem("hid_hi")
        s.hid_ready = sem("hid_ready")
        s.p_hi = sem("p_hi")
        s.p_ready = sem("p_ready")
        s.pz_ready = sem("pz_ready")
        s.pg_ready = sem("pg_ready")
        s.pm_ready = sem("pm_ready")
        s.z_ready = sem("z_ready")
        s.sig_done = sem("sig_done")
        s.fl_ready = sem("fl_ready")
        s.log_done = sem("log_done")
        s.k_ready = sem("k_ready")
        s.qg_ready = sem("qg_ready")
        s.suf_cleared = sem("suf_cleared")
        s.ex_done = sem("ex_done")
        s.cl_ready = sem("cl_ready")
        s.sums_step = sem("sums_step")
        s.hv_turned = sem("hv_turned")
        s.hv_copied = sem("hv_copied")
        s.diag_done = sem("diag_done")
        s.lvl_done = sem("lvl_done")
        s.am_step = sem("am_step")
        s.am_cleared = sem("am_cleared")
        s.ho_done = sem("ho_done")
        s.osq_done = sem("osq_done")
        s.o_summed = sem("o_summed")
        s.o_log = sem("o_log")
        s.o_rstd = sem("o_rstd")
        s.o_step = sem("o_step")
        ahead_act = [s.o_log, s.exp_done, s.qk_log, s.pt_copied, s.pg_ready, s.ex_done]
        ahead_dve = [s.masked, s.ox_ready, s.qk_scaled, s.q_roped, s.am_step, s.o_step]
        ahead_pool = [s.pm_ready, s.cl_ready, s.h_added]
        ahead_pe = [s.turned, s.o_done, s.ho_done, s.qk_summed, s.scored, s.lvl_done]
        block = ctx.enter_context(nc.Block())

        xin = x_t.rearrange("(k p) t -> p k t", p=P)
        pin = p_t.rearrange("l (k p) t -> l p k t", p=P)

        def pairs(t, m):
            return bass.AP(t, 0, [[2 * T, P], [2 * m, T // (2 * m)], [T + m, 2], [1, m]])

        def vraw(m):
            return (sm, dsum)[(m // 4) % 2][:, m % 4, :]

        def level_place(k):
            return ((6, k * P), (7, (k - 3) * P), (5, T + P))[[a <= k < b for a, b in GROUPS].index(True)]

        def conv_col(layer, tap, f):
            return f + (COLS["conv_w"] + (layer * 3 + tap) * FFT)

        @block.sync
        def _(sp):
            sp.dma_start(tab[:], table).then_inc(s.tab_in, 16)
            sp.dma_start(posi[:], positions.partition_broadcast(P).rearrange("p a t -> p (a t)")).then_inc(s.pos_in, 16)
            sp.dma_start(h[:, 0:4, :], xin[:, 0:4, :]).then_inc(s.x_in[0], 16)
            sp.dma_start(raw[:, 0, :], wstream[0]).then_inc(s.raw_in[0], 16)
            for k in range(1, 4):
                sp.dma_start(h[:, 4 * k:4 * k + 4, :], xin[:, 4 * k:4 * k + 4, :]).then_inc(s.x_in[k], 16)
            for u in range(1, 4):
                sp.dma_start(raw[:, u, :], wstream[u]).then_inc(s.raw_in[u], 16)
                if u == 1:
                    sp.dma_start(mat[:], mats).then_inc(s.mat_in, 16)
            sp.dma_start(lvlmask[:], masks).then_inc(s.mask_in, 16)

            def load(u):
                sp.wait_ge(s.lo_done, count((u - 4) * 2 + 2))
                src = wstream[bass.ds(u.v, 1)].rearrange("a p n -> p (a n)") if u.moving else wstream[u.c]
                sp.dma_start(raw[:, u.slot(4), :], src).then_inc(s.raw_in[u.slot(4)], 16)

            def load_range(a, b):
                n = (b - a) // 4
                with sp.Fori(0, n) as i:
                    for k in range(4):
                        load(Lin(a + k, 4, i))
                for u in range(a + 4 * n, b):
                    load(Lin(u))

            at_ = 4
            for layer in range(2):
                until = BASE[f"f{layer}"] + 1
                load_range(at_, until)
                sp.wait_ge(s.ox_ready, ahead(HEADS * (layer + 1)))
                sp.wait_ge(s.p_ready, count(layer))
                sp.dma_start(pt[:], pin[layer]).then_inc(s.p_in, 16)
                at_ = until
            load_range(at_, UNITS)
            for k in range(KT // 4):
                sp.wait_ge(s.h_added, ahead(2 * H_PER_LAYER - 16 + 4 * k + 4))
                sp.dma_start(out.rearrange("(k p) t -> p k t", p=P)[:, 4 * k:4 * k + 4, :], h[:, 4 * k:4 * k + 4, :]).then_inc(s.out_done, 16)
            sp.wait_ge(s.out_done, 64)

        @block.scalar
        def _(act):
            for a in ahead_act:
                act.sem_inc(a, AHEAD)

            def settle(idx):
                if isinstance(idx, Lin) and idx.moving:
                    act.sem_inc(s.gate_act)

            def split(u, halves=(0, 1)):
                act.wait_ge(s.raw_in[u.slot(4)], count(u.rounds(4) * 16 + 16))
                for k in halves:
                    act.wait_ge(s.quarter_done, count((u - 2) * 4 + 2 * k + 2))
                    act.activation(whi[:, u.slot(2), k * 1024:(k + 1) * 1024], raw[:, u.slot(4), k * 1024:(k + 1) * 1024],
                                   ACT.Copy).then_inc(s.hi_done, 1)

            def copy_p1(tile, quarter):
                act.wait_ge(s.quarter_done, count(quarter))
                act.wait_ge(s.evacuated, count(tile - 3))
                act.activation(p1[:, tile.slot(4), :], bank[tile.slot(4)][:, T:2 * T], ACT.Copy).then_inc(s.p1_copied, 1)

            def x_upper(gain, xbuf, kt):
                act.activation(row(xbuf, kt)[:, 0:T], row(h, kt), ACT.Copy, scale=col(tab, kt + gain)).then_inc(s.x_hi, 1)

            def x_square(nn, kt):
                n = kt + 16 * nn
                act.wait_ge(s.sq_added, count(n - 1))
                settle(kt)
                act.activation(sqb[:, n.slot(2), :], row(h, kt), ACT.Square).then_inc(s.sq_done, 1)

            def xprep(nn, gain, xbuf, kt, added):
                act.wait_ge(s.h_added, ahead(added))
                settle(kt)
                x_upper(gain, xbuf, kt)
                x_square(nn, kt)

            def norm(nn):
                act.wait_ge(s.norm_summed, count(nn + 1))
                act.activation(lnb[:], bank[4][:, 0:T], ACT.Ln, scale=1.0 / D, bias=eps[:, 0:1]).then_inc(s.norm_log, 1)
                act.wait_ge(s.norm_log, count(nn + 1))
                act.activation(rstd[:], lnb[:], ACT.Exp, scale=-0.5).then_inc(s.rstd_ready, 1)

            act.preload_act_table_set("natural_log_exp_and_others")
            act.wait_ge(s.tab_in, count(16))
            act.wait_ge(s.lb_dve, 1)
            act.activation(lb[:, 1:3, :], lb[:, 1:3, :], ACT.Exp).then_inc(s.lb_act, 1)
            for k in range(4):
                act.wait_ge(s.x_in[k], 16)
                for kt in range(4 * k, 4 * k + 4):
                    x_upper(COLS["mix"], xa, Lin(kt))
                if k == 0:
                    split(Lin(0))
            split(Lin(1))
            for kt in range(4):
                x_square(0, Lin(kt))

            def store_v(g):
                act.wait_ge(s.v_turned, count(g + 1))
                for t in range(2):
                    act.activation(vt[:, t, 512 * g:512 * g + 512], bank[4 + t][:], ACT.Copy).then_inc(s.v_stored, 1)

            for j in range(U_A):
                split(Lin(j + 2), (0,))
                copy_p1(Lin(j), Lin(4 * j + 4))
                split(Lin(j + 2), (1,))
                for kt in {0: range(4, 10), 1: range(10, KT)}.get(j, ()):
                    x_square(0, Lin(kt))
                if j == 2:
                    act.wait_ge(s.eps_set, 1)
                    norm(0)
                for m in {0: (), 1: (), 2: (0, 1, 2), 8: ()}.get(j, (j,)):
                    act.wait_ge(s.c_ready, count(m + 1))
                    act.wait_ge(s.cacc_done, count(m - 1))
                    act.activation(csq[:, m % 2, :], c[:, m, :], ACT.Square).then_inc(s.csq_done, 1)
                if j == 8:
                    act.wait_ge(s.rope_step, count(ROPE_STEPS))
                    act.activation(sinb[:], rr[:, 0, 3, :], ACT.Sin).then_inc(s.rope_ready, 1)
                    act.activation(cosb[:], rr[:, 1, 3, :], ACT.Sin).then_inc(s.rope_ready, 1)
                    act.preload_act_table_set("natural_log_exp_and_others")
                if j == 6:
                    act.wait_ge(s.c_summed, count(1))
                    act.activation(cln[:], bank[5][:, 0:T], ACT.Ln, scale=1.0 / 512, bias=eps[:, 0:1]).then_inc(s.c_log, 1)
                    act.wait_ge(s.c_log, count(1))
                    act.activation(rc[:, 0, :], cln[:], ACT.Exp, scale=-0.5).then_inc(s.rc_ready, 1)
                    for k in range(4):
                        act.wait_ge(s.cn_ready, count(k + 1))
                        act.activation(xc[:, k, 0:T], c[:, k, :], ACT.Copy, scale=tab[:, COLS["cq"] + k:COLS["cq"] + k + 1]).then_inc(s.xc_hi, 1)
            act.wait_ge(s.c_ready, count(9))
            act.activation(skpe[:], c[:, 8, :], ACT.Square).then_inc(s.skpe_done, 1)

            def squares(pr):
                act.wait_ge(s.qk_summed, ahead(pr * 2))
                settle(pr)
                for src, dst in ((qn, sqq), (kn, sqk)):
                    act.activation(dst[:], two(src, pr), ACT.Square).then_inc(s.q_squared, 1)
                act.activation(sqp[:], row(qp, pr), ACT.Square).then_inc(s.q_squared, 1)

            tile = TILE["q"]
            for n, u in enumerate(range(BASE["q"], BASE["o0"])):
                if n == U_Q + U_K + 2:
                    squares(Lin(0))
                if n == 1:
                    act.wait_ge(s.c_summed, count(2))
                    act.activation(cln[:], bank[5][:, T:2 * T], ACT.Ln, scale=1.0 / 512, bias=eps[:, 0:1]).then_inc(s.c_log, 1)
                    act.wait_ge(s.c_log, count(2))
                    act.activation(rc[:, 1, :], cln[:], ACT.Exp, scale=-0.5).then_inc(s.rc_ready, 1)
                for k in range(4):
                    copy_p1(Lin(tile), Lin(4 * u + k + 1))
                    tile += 1
                    if k % 2:
                        split(Lin(u + 2), (k // 2,))
                if n == 1:
                    for k in range(4, 8):
                        act.wait_ge(s.cn_ready, count(k + 1))
                        act.activation(xc[:, k, 0:T], c[:, k, :], ACT.Copy, scale=tab[:, COLS["cq"] + k:COLS["cq"] + k + 1]).then_inc(s.xc_hi, 1)
                g = n - (U_Q + U_K) - 1
                if g >= 0:
                    store_v(g)
            store_v(3)

            def qk_rms(pr, a):
                act.wait_ge(s.qk_summed, ahead(pr * 2 + a + 1))
                act.wait_ge(s.qk_scaled, ahead(pr * 6))
                act.activation(rqk[:, a, :, :], bank[6 + a][:].rearrange("p (w t) -> p w t", w=2), ACT.Ln, scale=1.0 / QK,
                               bias=eps[:, 0:1]).then_inc(s.qk_log, 1)
                act.wait_ge(s.qk_log, ahead(pr * 2 + a + 1))
                act.activation(rqk[:, a, :, :], rqk[:, a, :, :], ACT.Exp, scale=-0.5).then_inc(s.qk_rstd, 1)

            def exponentials(pr, a):
                hd = pr * 2 + a
                act.wait_ge(s.max_step, count(hd * 2 + 2))
                act.wait_ge(s.turned, ahead(hd - 1))
                for b in range(2):
                    act.activation(pb[:, a, b, 0:P * (b + 1)], ssb[:, a, b, 0:P * (b + 1)], ACT.Exp, scale=QK ** -0.5,
                                   bias=stat[:, a, 1, b:b + 1], accum_out=stat[:, a, 2, b:b + 1]).then_inc(s.exp_done, 1)

            def attend(pr, ahead_rms, ahead_squares):
                for a in range(2):
                    exponentials(pr, a)
                for a in range(2):
                    hd = pr * 2 + a
                    act.wait_ge(s.turned, ahead(hd + 1))
                    act.wait_ge(s.o_done, ahead(hd - 1))
                    act.activation(pts[:, a, :], bank[a][:, 0:3 * P], ACT.Copy).then_inc(s.pt_copied, 1)
                if ahead_squares:
                    squares(pr + 3)
                act.wait_ge(s.o_done, ahead(pr * 2 + 2))
                settle(pr)
                for a in range(2):
                    act.activation(row(xb, pr * 2 + a)[:, 0:T], bank[5][:, a * T:(a + 1) * T], ACT.Copy).then_inc(s.ox_hi, 1)
                if ahead_rms:
                    qk_rms(pr + 2, 0)
                    qk_rms(pr + 2, 1)

            for pr in range(2):
                qk_rms(Lin(pr), 0)
                qk_rms(Lin(pr), 1)
                squares(Lin(pr + 1))
            with act.Fori(0, PAIRS - 3) as i:
                attend(Lin(0, 1, i), True, True)
            attend(Lin(PAIRS - 3), True, False)
            attend(Lin(PAIRS - 2), False, False)
            attend(Lin(PAIRS - 1), False, False)

            def out_proj(layer):
                xbuf, nn = ((xa, 1), (xb, 4))[layer]
                u0, t0 = BASE[f"o{layer}"], TILE[f"o{layer}"]
                with act.Fori(0, KT // 4) as i:
                    for k in range(4):
                        split(Lin(u0 + k + 2, 4, i), (0,))
                        copy_p1(Lin(t0 + k, 4, i), Lin(4 * u0 + 4 * k + 4, 16, i))
                        split(Lin(u0 + k + 2, 4, i), (1,))
                        xprep(nn, COLS["ffn"] + KT * layer, xbuf, Lin(k, 4, i), Lin(layer * H_PER_LAYER + k + 1, 4, i))

            def ffn_pair(layer, f, u, tile, par, cpar, first=False):
                split(u + 2, (0,))
                copy_p1(tile, u * 4 + 4)
                split(u + 2, (1,))
                if first:
                    norm((1, 4)[layer])
                    act.preload_act_table(ACT.Silu)
                n = f + FFT * layer
                act.wait_ge(s.conv_done, count(n + 1))
                act.wait_ge(s.silu_scaled, count(n - 1))
                act.activation(sl[:, par, :], cv[:, 2, :], ACT.Silu).then_inc(s.silu_done, 1)
                split(u + 3, (0,))
                copy_p1(tile + 1, u * 4 + 8)
                split(u + 3, (1,))
                act.wait_ge(s.hid_done, count(n + 1))
                act.activation(hid[:, cpar, f.c % CH, 0:T], hv[:, par, :], ACT.Copy).then_inc(s.hid_hi, 1)

            def ffn(layer):
                u0, t0 = BASE[f"f{layer}"], TILE[f"f{layer}"]

                def operand(kt):
                    xprep((2, 5)[layer], COLS["ple"] + KT * layer, (xa, xb)[layer], Lin(kt), layer * H_PER_LAYER + 16 * NCH + kt + 1)

                for k in range(CH):
                    ffn_pair(layer, Lin(k), Lin(u0 + 2 * k), Lin(t0 + 2 * k), k % 2, 0, first=(k == 0))
                with act.Fori(0, (NCH - 1) // 2) as i:
                    for cc in range(2):
                        for k in range(CH):
                            u = Lin(u0 + 8 + 12 * cc + 3 * k, 24, i)
                            t = Lin(t0 + 8 + 24 * cc + 6 * k, 48, i)
                            ffn_pair(layer, Lin(4 + 4 * cc + k, 8, i), u, t, k % 2, (1 + cc) % 2)
                            for m in range(4):
                                copy_p1(t + (2 + m), (u + 2) * 4 + m + 1)
                                if m % 2:
                                    split(u + 4, (m // 2,))
                act.wait_ge(s.p_in, count(16 * (layer + 1)))
                act.activation(pts2[:, :, 0:T], pt[:], ACT.Copy).then_inc(s.p_hi, 1)
                for k in range(4):
                    for m in range(4):
                        copy_p1(Lin(t0 + 248 + 4 * k + m), Lin(4 * (u0 + 128 + k) + m + 1))
                        if m % 2:
                            split(Lin(u0 + 128 + k + 2), (m // 2,))
                        if k or m >= 2:
                            operand(4 * k + m - 2)
                operand(KT - 2)
                operand(KT - 1)

            def ple(layer):
                u0, t0 = BASE[f"pp{layer}"], TILE[f"pp{layer}"]
                for k in range(2):
                    for m in range(8):
                        copy_p1(Lin(t0 + 8 * k + m), Lin(4 * (u0 + k) + m // 2 + 1))
                        if m % 4 == 3:
                            split(Lin(u0 + k + 2), (m // 4,))
                u0, t0 = BASE[f"pg{layer}"], TILE[f"pg{layer}"]
                act.preload_act_table_set("natural_log_exp_and_others")
                norm((2, 5)[layer])
                act.preload_act_table(ACT.Sigmoid)

                def operand(kt):
                    xprep(3, COLS["mix"] + KT, xb, kt, kt + (H_PER_LAYER - 16 + 1))

                def body(i, k):
                    kt = Lin(k, 4, i) if i is not None else Lin(k)
                    tl, u = kt + t0, kt + u0
                    more = i is not None or k < KT - 2 or layer == 0
                    if more:
                        split(u + 2, (0,))
                    copy_p1(tl, u * 4 + 4)
                    if more:
                        split(u + 2, (1,))
                    n = kt + 16 * layer
                    act.wait_ge(s.pz_ready, count(n + 1))
                    act.wait_ge(s.pm_ready, ahead(n - 1))
                    act.activation(pg[:, k % 2, :], pz[:, k % 2, :], ACT.Sigmoid).then_inc(s.pg_ready, 1)
                    if layer == 0 and (i is not None or k):
                        operand(kt - 1)

                for k in range(4):
                    body(None, k)
                with act.Fori(0, KT // 4 - 2) as i:
                    for k in range(4, 8):
                        body(i, k)
                for k in range(KT - 4, KT):
                    body(None, k)
                if layer == 0:
                    operand(Lin(KT - 1))

            out_proj(0)
            ffn(0)
            ple(0)

            def levels(hd, a, b):
                for k in range(a, b):
                    n = hd * 8 + k
                    if k == 0:
                        act.wait_ge(s.log_done, count(hd + 1))
                        act.wait_ge(s.suf_cleared, count(hd + 1))
                    else:
                        act.wait_ge(s.sums_step, count(hd * 14 + 2 * k))
                    act.wait_ge(s.cl_ready, ahead(n - 1))
                    act.activation(ex[:, k % 2, :].rearrange("p (n g m) -> p n g m", g=2, m=1 << k), pairs(sufpre, 1 << k), ACT.Exp).then_inc(s.ex_done, 1)

            def head(hd, units, mix):
                u0, t0 = hd * 4 + BASE["h"], hd * 4 + TILE["h"]
                pv = hd - 1
                if mix:
                    levels(pv, LEAD, 4)
                if units:
                    split(u0 + 2, (0,))
                    copy_p1(t0, u0 * 4 + 4)
                if mix:
                    levels(pv, 4, 5)
                if units:
                    split(u0 + 2, (1,))
                if mix:
                    levels(pv, 5, 8)
                if units:
                    split(u0 + 3, (0,))
                    copy_p1(t0 + 1, u0 * 4 + 8)
                    split(u0 + 3, (1,))
                if mix:
                    act.wait_ge(s.hv_turned, count(pv + 1))
                    act.wait_ge(s.ho_done, ahead(pv))
                    act.activation(vtok[:], bank[4][:, 0:T].rearrange("p (a d) -> p a d", a=2), ACT.Copy).then_inc(s.hv_copied, 1)
                if units:
                    split(u0 + 4, (0,))
                    copy_p1(t0 + 2, u0 * 4 + 12)
                    split(u0 + 4, (1,))
                    act.wait_ge(s.z_ready, count(hd * 4 + 3))
                    act.wait_ge(s.qg_ready, count(hd * 2))
                    act.wait_ge(s.k_ready, count(hd))
                    act.activation(sg[:, 0:3, :], fqg[:], ACT.Sigmoid).then_inc(s.sig_done, 1)
                    act.activation(sg[:, 3, :], fqg[:, 0, :], ACT.Sigmoid, scale=-1.0).then_inc(s.sig_done, 1)
                if mix:
                    act.wait_ge(s.ho_done, ahead(pv + 1))
                    act.activation(osq[:], bank[4][:, T:2 * T], ACT.Square).then_inc(s.osq_done, 1)
                if units:
                    act.preload_act_table_set("natural_log_exp_and_others")
                    act.wait_ge(s.fl_ready, count(hd + 1))
                    act.wait_ge(s.cl_ready, ahead(hd * 8))
                    act.wait_ge(s.sums_step, count(hd * 14))
                    act.activation(sufpre[:, T:2 * T], fl[:], ACT.Ln).then_inc(s.log_done, 1)
                    levels(hd, 0, 1)
                    split(u0 + 5, (0,))
                    copy_p1(t0 + 3, u0 * 4 + 16)
                    levels(hd, 1, 2)
                    split(u0 + 5, (1,))
                    levels(hd, 2, LEAD)
                if mix:
                    act.wait_ge(s.o_summed, count(pv + 1))
                    act.activation(oln[:], bank[6][:, 0:T], ACT.Ln, scale=1.0 / P, bias=eps[:, 0:1]).then_inc(s.o_log, 1)
                    act.wait_ge(s.o_log, ahead(pv + 1))
                    act.activation(rso[:], oln[:], ACT.Exp, scale=-0.5).then_inc(s.o_rstd, 1)
                    act.wait_ge(s.o_step, ahead(pv * 2 + 2))
                    act.wait_ge(s.ox_ready, ahead(pv + (16 - 1)))
                    settle(pv)
                    act.activation(row(xa, pv)[:, 0:T], oy[:, 1, :], ACT.Copy).then_inc(s.ox_hi, 1)

            act.preload_act_table_set("natural_log_exp_and_others")
            u0, t0 = Lin(BASE["h"]), Lin(TILE["h"])
            split(u0 + 2, (0,))
            copy_p1(t0, u0 * 4 + 4)
            split(u0 + 2, (1,))
            norm(3)
            split(u0 + 3, (0,))
            copy_p1(t0 + 1, u0 * 4 + 8)
            split(u0 + 3, (1,))
            split(u0 + 4, (0,))
            copy_p1(t0 + 2, u0 * 4 + 12)
            split(u0 + 4, (1,))
            act.wait_ge(s.z_ready, count(3))
            act.activation(sg[:, 0:3, :], fqg[:], ACT.Sigmoid).then_inc(s.sig_done, 1)
            act.activation(sg[:, 3, :], fqg[:, 0, :], ACT.Sigmoid, scale=-1.0).then_inc(s.sig_done, 1)
            act.preload_act_table_set("natural_log_exp_and_others")
            act.wait_ge(s.fl_ready, count(1))
            act.activation(sufpre[:, T:2 * T], fl[:], ACT.Ln).then_inc(s.log_done, 1)
            levels(Lin(0), 0, 1)
            split(u0 + 5, (0,))
            copy_p1(t0 + 3, u0 * 4 + 16)
            levels(Lin(0), 1, 2)
            split(u0 + 5, (1,))
            levels(Lin(0), 2, LEAD)
            with act.Fori(0, HEADS - 1) as i:
                head(Lin(1, 1, i), True, True)
            head(Lin(HEADS), False, True)

            out_proj(1)
            ffn(1)
            ple(1)

        @block.vector
        def _(dve):
            for a in ahead_dve:
                dve.sem_inc(a, AHEAD)

            def split(u, halves=(0, 1)):
                for k in halves:
                    dve.wait_ge(s.hi_done, count(u * 2 + k + 1))
                    cols = slice(k * 1024, (k + 1) * 1024)
                    dve.tensor_tensor(wlo[:, u.slot(2), cols], raw[:, u.slot(4), cols], whi[:, u.slot(2), cols].bitcast(F32),
                                      ALU.subtract).then_inc(s.lo_done, 1)

            def whole(tile, dst):
                dve.wait_ge(s.p1_copied, count(tile + 1))
                dve.tensor_tensor(dst, bank[tile.slot(4)][:, 0:T], p1[:, tile.slot(4), :], ALU.add).then_inc(s.evacuated, 1)

            def whole_scaled(tile, dst, nn, done):
                whole(tile, sm[:, tile.slot(4), :])
                scaled(tile, dst, nn, done)

            def scaled(tile, dst, nn, done):
                dve.wait_ge(s.evacuated, count(tile + 1))
                dve.wait_ge(s.rstd_ready, count(nn + 1))
                dve.tensor_tensor(dst, sm[:, tile.slot(4), :], rstd[:], ALU.mult).then_inc(done, 1)

            def to_residual(tile, n):
                dve.wait_ge(s.h_added, ahead(n - 3))
                whole(tile, dsum[:, n.slot(4), :])

            def xprep(nn, gain, xbuf, kt):
                n = kt + 16 * nn
                dve.wait_ge(s.x_hi, count(n + 1))
                dve.scalar_tensor_tensor(row(xbuf, kt)[:, T:2 * T], row(h, kt), col(tab, kt + gain), row(xbuf, kt)[:, 0:T].bitcast(F32),
                                         ALU.mult, ALU.subtract).then_inc(s.x_ready, 1)

            dve.memset(eps[:], EPS).then_inc(s.eps_set, 1)
            rope = [0]

            def step(ins):
                ins.then_inc(s.rope_step, 1)
                rope[0] += 1
                dve.wait_ge(s.rope_step, rope[0])

            def rotary(k):
                two_pi = 2.0 * np.pi
                c1 = 6.28125
                c2 = float(np.float32(np.round((two_pi - c1) * 2.0 ** 21) / 2.0 ** 21))
                c3 = float(two_pi - c1 - c2)
                magic = 12582912.0
                turn, shift = ((0.0, 0.0), (0.25, float(np.pi / 2)))[k]
                if k == 0:
                    dve.wait_ge(s.pos_in, 16)
                    step(dve.tensor_copy(kk[:, 0, :], posi[:]))
                    step(dve.tensor_scalar(ang[:], kk[:, 0, :], tab[:, COLS["inv_freq"]:COLS["inv_freq"] + 1], None, ALU.mult))
                step(dve.tensor_scalar(rr[:, k, 0, :], ang[:], float(1 / two_pi), turn, ALU.mult, ALU.add))
                step(dve.tensor_scalar(rr[:, k, 1, :], rr[:, k, 0, :], magic, None, ALU.add))
                step(dve.tensor_scalar(kk[:, k, :], rr[:, k, 1, :], -magic, None, ALU.add))
                step(dve.scalar_tensor_tensor(rr[:, k, 0, :], kk[:, k, :], -c1, ang[:], ALU.mult, ALU.add))
                step(dve.scalar_tensor_tensor(rr[:, k, 1, :], kk[:, k, :], -c2, rr[:, k, 0, :], ALU.mult, ALU.add))
                step(dve.scalar_tensor_tensor(rr[:, k, 2, :], kk[:, k, :], -c3, rr[:, k, 1, :], ALU.mult, ALU.add))
                step(dve.tensor_scalar(rr[:, k, 0, :], rr[:, k, 2, :], shift, float(np.float32(3.1415925)), ALU.add, ALU.min))
                step(dve.tensor_scalar(rr[:, k, 3, :], rr[:, k, 0, :], float(np.float32(-3.1415925)), None, ALU.max))

            def bounds():
                l0 = tab[:, COLS["logit0"]:COLS["logit0"] + 16]
                l1 = tab[:, COLS["logit1"]:COLS["logit1"] + 16]
                step(dve.tensor_tensor(lb[:, 0, :], l0, l1, ALU.max))
                step(dve.tensor_tensor(lb[:, 1, :], l0, lb[:, 0, :], ALU.subtract))
                dve.tensor_tensor(lb[:, 2, :], l1, lb[:, 0, :], ALU.subtract).then_inc(s.lb_dve, 1)

            def bounds_rest():
                dve.wait_ge(s.lb_act, 1)
                step(dve.tensor_tensor(lb[:, 0, :], lb[:, 1, :], lb[:, 2, :], ALU.add))
                step(dve.reciprocal(lb[:, 3, :], lb[:, 0, :]))
                step(dve.tensor_tensor(lb[:, 1, :], lb[:, 1, :], lb[:, 3, :], ALU.mult))
                step(dve.tensor_tensor(lb[:, 2, :], lb[:, 2, :], lb[:, 3, :], ALU.mult))
                step(dve.tensor_tensor(lb[:, 0, :], lb[:, 1, :], lb[:, 2, :], ALU.add))
                step(dve.tensor_tensor(lb[:, 2, :], lb[:, 0, :], lb[:, 1, :], ALU.subtract))
                step(dve.tensor_scalar(lb[:, 3, :], lb[:, 2, :], -1.0, 1.0, ALU.mult, ALU.add))

            def c_scale(k, rcol, need):
                dve.wait_ge(s.rc_ready, count(need))
                dve.tensor_tensor(c[:, k, :], c[:, k, :], rc[:, rcol, :], ALU.mult).then_inc(s.cn_ready, 1)

            def c_lower(k):
                dve.wait_ge(s.xc_hi, count(k + 1))
                dve.scalar_tensor_tensor(xc[:, k, T:2 * T], c[:, k, :], tab[:, COLS["cq"] + k:COLS["cq"] + k + 1], xc[:, k, 0:T].bitcast(F32),
                                         ALU.mult, ALU.subtract).then_inc(s.xc_ready, 1)

            dve.wait_ge(s.tab_in, 16)
            bounds()
            for kt in range(KT):
                xprep(0, COLS["mix"], xa, Lin(kt))
                if kt == 3:
                    split(Lin(0))
            split(Lin(1))
            bounds_rest()

            for j in range(U_A):
                split(Lin(j + 2), (0,))
                whole(Lin(j), sm[:, j % 4, :])
                split(Lin(j + 2), (1,))
                for m in {0: (), 1: (), 2: (0, 1, 2)}.get(j, (j,)):
                    scaled(Lin(m), c[:, m, :], 0, s.c_ready)
                if j in (0, 5):
                    rotary(j // 5)
                if j == 5:
                    assert rope[0] == ROPE_STEPS
                if j == 6:
                    for k in range(4):
                        dve.wait_ge(s.csq_done, count(k + 1))
                        c_scale(k, 0, 1)
                    for k in range(4):
                        c_lower(k)
            dve.wait_ge(s.c_ready, count(9))
            dve.tensor_scalar(kg[:], c[:, 8, :], tab[:, COLS["gk_pe"]:COLS["gk_pe"] + 1], None, ALU.mult).then_inc(s.kg_ready, 1)

            dve.wait_ge(s.rope_ready, 2)
            tile = TILE["q"]
            for n, u in enumerate(range(BASE["q"], BASE["o0"])):
                for k in range(4):
                    m = 4 * n + k
                    if m < 16:
                        dst = qn[:, m, :]
                    elif m < 24:
                        dst = qp[:, m - 16, :]
                    elif m < 40:
                        dst = kn[:, m - 24, :]
                    else:
                        dve.wait_ge(s.v_turned, count((m - 40) // 4 - 1))
                        dst = vraw(m - 40)
                    whole(Lin(tile), dst)
                    tile += 1
                    if k % 2:
                        split(Lin(u + 2), (k // 2,))
                if n == 1:
                    for k in range(4, 8):
                        dve.wait_ge(s.csq_done, count(k + 1))
                        c_scale(k, 1, 2)
                    for k in range(4, 8):
                        c_lower(k)
                if n == 3:
                    dve.wait_ge(s.k_rotated, 1)
                    dve.wait_ge(s.rope_ready, 2)
                    dve.tensor_tensor(kr[:, 0, :], bank[6][:, 0:T], sinb[:], ALU.mult).then_inc(s.k_roped, 1)
                    dve.tensor_tensor(kr[:, 1, :], kg[:], cosb[:], ALU.mult).then_inc(s.k_roped, 1)
                    dve.wait_ge(s.k_roped, 2)
                    dve.tensor_tensor(kro[:], kr[:, 0, :], kr[:, 1, :], ALU.add).then_inc(s.k_roped, 1)

            gain = {n: tab[:, COLS[n]:COLS[n] + 1] for n in ("gq_nope", "gq_pe", "gk_nope", "gk_pe")}

            def scale_q_rope(pr):
                dve.wait_ge(s.qk_rstd, count(pr * 2 + 2))
                dve.wait_ge(s.q_roped, ahead(pr))
                for a in range(2):
                    half = slice(64 * a, 64 * a + 64)
                    dve.scalar_tensor_tensor(qps[half, :], half_row(qp, half, pr), gain["gq_pe"][half], rq[half, a, :],
                                             ALU.mult, ALU.mult).then_inc(s.qk_scaled, 1)

            def scale_q_k(pr):
                dve.wait_ge(s.scored, ahead(pr * 2))
                dve.scalar_tensor_tensor(qs[:], two(qn, pr), gain["gq_nope"], rq, ALU.mult, ALU.mult).then_inc(s.qk_scaled, 1)
                dve.scalar_tensor_tensor(ks[:], two(kn, pr), gain["gk_nope"], rk, ALU.mult, ALU.mult).then_inc(s.qk_scaled, 1)
                for a in range(2):
                    half = slice(64 * a, 64 * a + 64)
                    dve.tensor_tensor(kps[half, :], kro[half, :], rk[half, a, :], ALU.mult).then_inc(s.qk_scaled, 1)

            def rope_q(pr):
                dve.wait_ge(s.q_rotated, count(pr + 1))
                dve.tensor_tensor(rt[:, 0, :], bank[2][:, 0:T], sinb[:], ALU.mult).then_inc(s.q_parts, 1)
                dve.wait_ge(s.q_parts, count(pr + 1))
                dve.wait_ge(s.q_cos, count(pr + 1))
                dve.tensor_tensor(qpr[:], rt[:, 0, :], rt[:, 1, :], ALU.add).then_inc(s.q_roped, 1)

            def maxima(pr, a):
                hd = pr * 2 + a
                dve.wait_ge(s.scored, ahead(hd + 1))
                dve.wait_ge(s.exp_done, ahead(hd * 2 - 2))
                if a == 0:
                    dve.wait_ge(s.masked, ahead(pr * 6 + 1))
                dve.tensor_tensor(ssb[:, a, 0, 0:P], bank[3 + a][:, 0:P], tri, ALU.add).then_inc(s.masked, 1)
                dve.tensor_copy(ssb[:, a, 1, 0:P], bank[3 + a][:, P:2 * P]).then_inc(s.masked, 1)
                dve.tensor_tensor(ssb[:, a, 1, P:2 * P], bank[3 + a][:, 2 * P:3 * P], tri, ALU.add).then_inc(s.masked, 1)
                dve.wait_ge(s.masked, ahead(hd * 3 + 4))
                dve.tensor_reduce(stat[:, a, 0, :], ssb[:, a, :, :], AX.X, ALU.max).then_inc(s.max_step, 1)
                dve.wait_ge(s.max_step, count(hd * 2 + 1))
                dve.tensor_scalar(stat[:, a, 1, :], stat[:, a, 0, :], -(QK ** -0.5), None, ALU.mult).then_inc(s.max_step, 1)

            def probabilities(pr, a):
                hd = pr * 2 + a
                dve.wait_ge(s.exp_done, ahead(hd * 2 + 2))
                dve.reciprocal(stat[:, a, 3, :], stat[:, a, 2, :]).then_inc(s.probs_step, 1)
                dve.wait_ge(s.probs_step, count(hd + 1))
                for b in range(2):
                    dve.tensor_scalar(pb[:, a, b, 0:P * (b + 1)], pb[:, a, b, 0:P * (b + 1)], stat[:, a, 3, b:b + 1], None,
                                      ALU.mult).then_inc(s.probs_ready, 1)

            def attend(pr, nxt):
                maxima(pr, 0)
                if nxt:
                    scale_q_rope(pr + 1)
                maxima(pr, 1)
                probabilities(pr, 0)
                probabilities(pr, 1)
                if nxt:
                    scale_q_k(pr + 1)
                    rope_q(pr + 1)
                for a in range(2):
                    dve.wait_ge(s.ox_hi, count(pr * 2 + 2))
                    dve.tensor_tensor(row(xb, pr * 2 + a)[:, T:2 * T], bank[5][:, a * T:(a + 1) * T], row(xb, pr * 2 + a)[:, 0:T].bitcast(F32),
                                      ALU.subtract).then_inc(s.ox_ready, 1)

            scale_q_rope(Lin(0))
            scale_q_k(Lin(0))
            rope_q(Lin(0))
            dve.memset(sm[:], NEG).then_inc(s.masked, 1)
            with dve.Fori(0, PAIRS - 1) as i:
                attend(Lin(0, 1, i), True)
            attend(Lin(PAIRS - 1), False)

            def out_proj(layer):
                xbuf, nn = ((xa, 1), (xb, 4))[layer]
                u0, t0 = BASE[f"o{layer}"], TILE[f"o{layer}"]
                with dve.Fori(0, KT // 4) as i:
                    for k in range(4):
                        split(Lin(u0 + k + 2, 4, i), (0,))
                        to_residual(Lin(t0 + k, 4, i), Lin(layer * H_PER_LAYER + k, 4, i))
                        split(Lin(u0 + k + 2, 4, i), (1,))
                        xprep(nn, COLS["ffn"] + KT * layer, xbuf, Lin(k, 4, i))

            def gate_post(layer, f, tile, par):
                n = f + FFT * layer
                nn = (1, 4)[layer]
                w = [col(tab, conv_col(layer, tap, f)) for tap in range(3)]
                b = col(tab, f + (COLS["conv_b"] + layer * FFT))
                whole_scaled(tile, gn[:, par, 2:T + 2], nn, s.gate_scaled)
                dve.wait_ge(s.gate_scaled, count(n + 1))
                dve.tensor_scalar(cv[:, 0, :], gn[:, par, 2:T + 2], w[2], b, ALU.mult, ALU.add).then_inc(s.conv_step, 1)
                dve.wait_ge(s.conv_step, count(n * 2 + 1))
                dve.scalar_tensor_tensor(cv[:, 1, :], gn[:, par, 1:T + 1], w[1], cv[:, 0, :], ALU.mult, ALU.add).then_inc(s.conv_step, 1)
                dve.wait_ge(s.conv_step, count(n * 2 + 2))
                dve.wait_ge(s.silu_done, count(n))
                dve.scalar_tensor_tensor(cv[:, 2, :], gn[:, par, 0:T], w[0], cv[:, 1, :], ALU.mult, ALU.add).then_inc(s.conv_done, 1)

            def up_post(layer, f, tile, par):
                n = f + FFT * layer
                whole(tile, sm[:, tile.slot(4), :])
                dve.wait_ge(s.evacuated, count(tile + 1))
                dve.wait_ge(s.silu_scaled, count(n + 1))
                dve.wait_ge(s.hid_ready, count(n - 1))
                dve.tensor_tensor(hv[:, par, :], sm[:, tile.slot(4), :], slr[:, par, :], ALU.mult).then_inc(s.hid_done, 1)

            def hid_lower(layer, f, par, cpar):
                n = f + FFT * layer
                dve.wait_ge(s.hid_hi, count(n + 1))
                dve.tensor_tensor(hid[:, cpar, f.c % CH, T:2 * T], hv[:, par, :], hid[:, cpar, f.c % CH, 0:T].bitcast(F32),
                                  ALU.subtract).then_inc(s.hid_ready, 1)

            def ffn(layer):
                u0, t0 = BASE[f"f{layer}"], TILE[f"f{layer}"]
                hb = layer * H_PER_LAYER + 16

                def operand(kt):
                    xprep((2, 5)[layer], COLS["ple"] + KT * layer, (xa, xb)[layer], Lin(kt))

                dve.wait_ge(s.gate_scaled, count(FFT * layer))
                dve.memset(gn[:, :, 0:2], 0.0).then_inc(s.pads_set, 1)
                dve.wait_ge(s.pads_set, layer + 1)
                for k in range(CH):
                    u, t, f = Lin(u0 + 2 * k), Lin(t0 + 2 * k), Lin(k)
                    split(u + 2, (0,))
                    gate_post(layer, f, t, k % 2)
                    split(u + 2, (1,))
                    split(u + 3, (0,))
                    up_post(layer, f, t + 1, k % 2)
                    split(u + 3, (1,))
                    hid_lower(layer, f, k % 2, 0)
                with dve.Fori(0, (NCH - 1) // 2) as i:
                    for cc in range(2):
                        for k in range(CH):
                            u = Lin(u0 + 8 + 12 * cc + 3 * k, 24, i)
                            t = Lin(t0 + 8 + 24 * cc + 6 * k, 48, i)
                            f = Lin(4 + 4 * cc + k, 8, i)
                            split(u + 2, (0,))
                            gate_post(layer, f, t, k % 2)
                            split(u + 2, (1,))
                            split(u + 3, (0,))
                            up_post(layer, f, t + 1, k % 2)
                            split(u + 3, (1,))
                            hid_lower(layer, f, k % 2, (1 + cc) % 2)
                            for m in range(4):
                                to_residual(t + (2 + m), Lin(hb + 16 * cc + 4 * k + m, 32, i))
                                if m % 2:
                                    split(u + 4, (m // 2,))
                dve.wait_ge(s.p_hi, count(layer + 1))
                dve.tensor_tensor(pts2[:, :, T:2 * T], pt[:], pts2[:, :, 0:T].bitcast(F32), ALU.subtract).then_inc(s.p_ready, 1)
                for k in range(4):
                    for m in range(4):
                        kt = 4 * k + m
                        to_residual(Lin(t0 + 248 + kt), Lin(hb + 16 * (NCH - 1) + kt))
                        if m % 2:
                            split(Lin(u0 + 128 + k + 2), (m // 2,))
                        if kt >= 2:
                            operand(kt - 2)
                operand(KT - 2)
                operand(KT - 1)

            def ple(layer):
                u0, t0 = BASE[f"pp{layer}"], TILE[f"pp{layer}"]
                for k in range(2):
                    for m in range(8):
                        whole(Lin(t0 + 8 * k + m), pp[:, 8 * k + m, :])
                        if m % 4 == 3:
                            split(Lin(u0 + k + 2), (m // 4,))
                u0, t0 = BASE[f"pg{layer}"], TILE[f"pg{layer}"]

                def operand(kt):
                    xprep(3, COLS["mix"] + KT, xb, kt)

                def body(i, k):
                    kt = Lin(k, 4, i) if i is not None else Lin(k)
                    tl, u = kt + t0, kt + u0
                    more = i is not None or k < KT - 2 or layer == 0
                    if more:
                        split(u + 2, (0,))
                    dve.wait_ge(s.pg_ready, ahead(kt + (16 * layer - 1)))
                    whole_scaled(tl, pz[:, k % 2, :], (2, 5)[layer], s.pz_ready)
                    if more:
                        split(u + 2, (1,))
                    if layer == 0 and (i is not None or k):
                        operand(kt - 1)

                for k in range(4):
                    body(None, k)
                with dve.Fori(0, KT // 4 - 2) as i:
                    for k in range(4, 8):
                        body(i, k)
                for k in range(KT - 4, KT):
                    body(None, k)
                if layer == 0:
                    operand(Lin(KT - 1))

            out_proj(0)
            ffn(0)
            ple(0)

            def sums(hd, a, b):
                for k in range(a, b):
                    m = 1 << k
                    sv = sufpre[:, 0:T].rearrange("p (n g m) -> p n g m", g=2, m=m)
                    pv_ = sufpre[:, T:2 * T].rearrange("p (n g m) -> p n g m", g=2, m=m)
                    nb = T // (2 * m)
                    dve.wait_ge(s.ex_done, ahead(hd * 8 + k + 1))
                    if k:
                        dve.wait_ge(s.sums_step, count(hd * 14 + 2 * k))
                    dve.tensor_tensor(sv[:, :, 0, :], sv[:, :, 0, :], pv_[:, :, 1, m - 1:m].to_broadcast([P, nb, m]), ALU.add).then_inc(s.sums_step, 1)
                    dve.wait_ge(s.sums_step, count(hd * 14 + 2 * k + 1))
                    dve.tensor_tensor(pv_[:, :, 1, :], pv_[:, :, 1, :], pv_[:, :, 0, m - 1:m].to_broadcast([P, nb, m]), ALU.add).then_inc(s.sums_step, 1)

            def place_level(k):
                m = 1 << k
                b, o = level_place(k)
                dve.copy_predicated(bass.AP(am, m, [[3 * P, P], [2 * P, 2], [2 * m, P // (2 * m)], [1, m]]),
                                    lvlmask[:, k * P:(k + 1) * P].rearrange("p (t n m) -> p t n m", t=2, m=m),
                                    bank[b][:, o:o + P].rearrange("p (t n m) -> p t n m", t=2, m=m)).then_inc(s.am_step, 1)

            def place_levels(pv, a, b):
                dve.wait_ge(s.lvl_done, ahead(pv * len(GROUPS) + GROUPS.index((a, b)) + 1))
                for k in range(a, min(b, LEVELS)):
                    dve.wait_ge(s.am_step, ahead(pv * 9 + k + 1))
                    dve.sem_inc(s.gate_dve)
                    place_level(k)

            def head(hd, units, mix):
                u0, t0 = hd * 4 + BASE["h"], hd * 4 + TILE["h"]
                pv = hd - 1
                if mix:
                    sums(pv, LEAD, 4)
                if units:
                    split(u0 + 2, (0,))
                    dve.wait_ge(s.z_ready, count(hd * 4 - 3))
                    whole(t0, sm[:, t0.slot(4), :])
                if mix:
                    sums(pv, 4, 5)
                if units:
                    split(u0 + 2, (1,))
                if mix:
                    sums(pv, 5, 7)
                    dve.wait_ge(s.diag_done, count(pv + 1))
                    dve.wait_ge(s.ho_done, ahead(pv))
                    dve.sem_inc(s.gate_dve)
                    dve.copy_predicated(bass.AP(am, 0, [[3 * P, P], [2 * P, 2], [1, P]]),
                                        lvlmask[:, LEVELS * P:].rearrange("p (t n) -> p t n", t=2),
                                        bank[5][:, 0:T].rearrange("p (t n) -> p t n", t=2)).then_inc(s.am_step, 1)
                    place_levels(pv, *GROUPS[0])
                if units:
                    split(u0 + 3, (0,))
                    dve.wait_ge(s.z_ready, count(hd * 4 - 2))
                    whole(t0 + 1, sm[:, (t0 + 1).slot(4), :])
                    split(u0 + 3, (1,))
                if mix:
                    place_levels(pv, *GROUPS[1])
                if units:
                    split(u0 + 4, (0,))
                    dve.wait_ge(s.z_ready, count(hd * 4 - 1))
                    whole(t0 + 2, sm[:, (t0 + 2).slot(4), :])
                if mix:
                    place_levels(pv, *GROUPS[2])
                    dve.wait_ge(s.am_step, ahead(pv * 9 + 8))
                    dve.tensor_copy(am[:, 1, :], bank[5][:, T:T + P]).then_inc(s.am_step, 1)
                if units:
                    split(u0 + 4, (1,))
                    gates(hd)
                    sums(hd, 0, 1)
                    split(u0 + 5, (0,))
                    dve.wait_ge(s.z_ready, count(hd * 4))
                    whole(t0 + 3, sm[:, (t0 + 3).slot(4), :])
                    sums(hd, 1, 2)
                    split(u0 + 5, (1,))
                    sums(hd, 2, LEAD)
                if mix:
                    dve.wait_ge(s.o_rstd, count(pv + 1))
                    dve.tensor_tensor(oy[:, 0, :], bank[4][:, T:2 * T], rso[:], ALU.mult).then_inc(s.o_step, 1)
                    dve.wait_ge(s.o_step, ahead(pv * 2 + 1))
                    dve.wait_ge(s.qg_ready, count(pv * 2 + 2))
                    dve.scalar_tensor_tensor(oy[:, 1, :], oy[:, 0, :], col(tab, pv + COLS["o_norm"]), gs[:], ALU.mult,
                                             ALU.mult).then_inc(s.o_step, 1)
                    dve.wait_ge(s.ox_hi, count(pv + (16 + 1)))
                    dve.tensor_tensor(row(xa, pv)[:, T:2 * T], oy[:, 1, :], row(xa, pv)[:, 0:T].bitcast(F32), ALU.subtract).then_inc(s.ox_ready, 1)

            def lb_col(k, hd):
                return col(lb[:, k, :], hd)

            def gates(hd):
                dve.wait_ge(s.sig_done, count(hd * 2 + 1))
                dve.wait_ge(s.log_done, count(hd))
                dve.tensor_scalar(fl[:], sg[:, 0, :], lb_col(3, hd), lb_col(2, hd), ALU.mult, ALU.add).then_inc(s.fl_ready, 1)
                dve.wait_ge(s.sig_done, count(hd * 2 + 2))
                dve.wait_ge(s.cl_ready, ahead(hd * 8))
                dve.wait_ge(s.diag_done, count(hd))
                dve.tensor_scalar(kq[:, 0:T], sg[:, 3, :], lb_col(3, hd), None, ALU.mult).then_inc(s.k_ready, 1)
                dve.wait_ge(s.ex_done, ahead(hd * 8))
                dve.wait_ge(s.sums_step, count(hd * 14))
                dve.memset(sufpre[:, 0:T], 0.0).then_inc(s.suf_cleared, 1)

            dve.wait_ge(s.h_added, ahead(H_PER_LAYER))
            dve.memset(am[:], 0.0).then_inc(s.am_cleared, 1)
            dve.wait_ge(s.mask_in, 16)
            dve.wait_ge(s.am_cleared, 1)
            head(Lin(0), True, False)
            with dve.Fori(0, HEADS - 1) as i:
                head(Lin(1, 1, i), True, True)
            head(Lin(HEADS), False, True)

            out_proj(1)
            ffn(1)
            ple(1)

        @block.gpsimd
        def _(pool):
            for a in ahead_pool:
                pool.sem_inc(a, AHEAD)

            def settle(idx):
                if idx.moving:
                    pool.sem_inc(s.gate_pool)

            def xsquare(nn, kt):
                n = kt + 16 * nn
                pool.wait_ge(s.sq_done, count(n + 1))
                if not kt.moving and kt.c == 0:
                    pool.wait_ge(s.norm_summed, count(nn))
                    pool.tensor_copy(sqacc[:], sqb[:, 0, :]).then_inc(s.sq_added, 1)
                else:
                    pool.wait_ge(s.sq_added, count(n))
                    pool.tensor_tensor(sqacc[:], sqacc[:], sqb[:, n.slot(2), :], ALU.add).then_inc(s.sq_added, 1)

            def to_residual(tile, n, kt):
                pool.wait_ge(s.evacuated, count(tile + 1))
                pool.wait_ge(s.h_added, ahead(n))
                settle(kt)
                pool.tensor_tensor(row(h, kt), row(h, kt), dsum[:, n.slot(4), :], ALU.add).then_inc(s.h_added, 1)

            for kt in range(KT):
                xsquare(0, Lin(kt))
            for j in range(8):
                pool.wait_ge(s.csq_done, count(j + 1))
                if j % 4 == 0:
                    pool.tensor_copy(cacc[:, j // 4, :], csq[:, j % 2, :]).then_inc(s.cacc_done, 1)
                else:
                    pool.wait_ge(s.cacc_done, count(j))
                    pool.tensor_tensor(cacc[:, j // 4, :], cacc[:, j // 4, :], csq[:, j % 2, :], ALU.add).then_inc(s.cacc_done, 1)

            def q_cosines(pr):
                pool.wait_ge(s.qk_scaled, ahead(pr * 6 + 2))
                pool.wait_ge(s.q_roped, ahead(pr))
                pool.tensor_tensor(rt[:, 1, :], qps[:], cosb[:], ALU.mult).then_inc(s.q_cos, 1)

            def attend(pr, nxt):
                pool.wait_ge(s.o_done, ahead(pr * 2))
                pool.wait_ge(s.v_stored, count(8))
                pool.sem_inc(s.gate_pool)
                values = slice(pr.c * 256, pr.c * 256 + 256) if not pr.moving else bass.ds((pr * 256).v, 256)
                pool.tensor_copy(vs[:], vt[:, :, values]).then_inc(s.v_picked, 1)
                if nxt:
                    q_cosines(pr + 1)

            q_cosines(Lin(0))
            with pool.Fori(0, PAIRS - 1) as i:
                attend(Lin(0, 1, i), True)
            attend(Lin(PAIRS - 1), False)

            def out_proj(layer):
                nn = (1, 4)[layer]
                t0 = TILE[f"o{layer}"]
                pool.wait_ge(s.norm_summed, nn)
                pool.memset(sqacc[:], 0.0).then_inc(s.sq_clear, 1)
                pool.wait_ge(s.sq_clear, {1: 1, 3: 2, 4: 3}[nn])
                with pool.Fori(0, KT // 4) as i:
                    for k in range(4):
                        kt = Lin(k, 4, i)
                        to_residual(Lin(t0 + k, 4, i), kt + layer * H_PER_LAYER, kt)
                        xsquare_add(nn, kt)

            def xsquare_add(nn, kt):
                n = kt + 16 * nn
                pool.wait_ge(s.sq_done, count(n + 1))
                pool.wait_ge(s.sq_added, count(n))
                pool.tensor_tensor(sqacc[:], sqacc[:], sqb[:, n.slot(2), :], ALU.add).then_inc(s.sq_added, 1)

            def silu_scale(layer, f, par):
                n = f + FFT * layer
                pool.wait_ge(s.silu_done, count(n + 1))
                pool.wait_ge(s.hid_done, count(n - 1))
                pool.wait_ge(s.rstd_ready, count((1, 4)[layer] + 1))
                pool.tensor_tensor(slr[:, par, :], sl[:, par, :], rstd[:], ALU.mult).then_inc(s.silu_scaled, 1)

            def ffn(layer):
                u0, t0 = BASE[f"f{layer}"], TILE[f"f{layer}"]
                hb = layer * H_PER_LAYER + 16
                for k in range(CH):
                    silu_scale(layer, Lin(k), k % 2)
                with pool.Fori(0, (NCH - 1) // 2) as i:
                    for cc in range(2):
                        for k in range(CH):
                            t = Lin(t0 + 8 + 24 * cc + 6 * k, 48, i)
                            silu_scale(layer, Lin(4 + 4 * cc + k, 8, i), k % 2)
                            for m in range(4):
                                to_residual(t + (2 + m), Lin(hb + 16 * cc + 4 * k + m, 32, i), Lin(4 * k + m))
                for kt in range(KT + 3):
                    if kt < KT:
                        to_residual(Lin(t0 + 248 + kt), Lin(hb + 16 * (NCH - 1) + kt), Lin(kt))
                    if kt >= 3:
                        xsquare((2, 5)[layer], Lin(kt - 3))

            def ple(layer):
                nn = 3
                if layer == 0:
                    pool.wait_ge(s.norm_summed, nn)
                    pool.memset(sqacc[:], 0.0).then_inc(s.sq_clear, 1)
                    pool.wait_ge(s.sq_clear, {1: 1, 3: 2, 4: 3}[nn])
                with pool.Fori(0, KT // 4) as i:
                    for k in range(4):
                        kt = Lin(k, 4, i)
                        n = kt + 16 * layer
                        pool.wait_ge(s.pg_ready, ahead(n + 1))
                        pool.wait_ge(s.evacuated, count(TILE[f"pg{layer}"]))
                        settle(kt)
                        pool.tensor_tensor(pm[:, k % 2, :], pg[:, k % 2, :], row(pp, kt), ALU.mult).then_inc(s.pm_ready, 1)
                        pool.wait_ge(s.pm_ready, ahead(n + 1))
                        hn = kt + ((layer + 1) * H_PER_LAYER - 16)
                        pool.wait_ge(s.h_added, ahead(hn))
                        settle(kt)
                        pool.tensor_tensor(row(h, kt), row(h, kt), pm[:, k % 2, :], ALU.add).then_inc(s.h_added, 1)
                        if layer == 0:
                            xsquare_add(nn, kt)

            out_proj(0)
            ffn(0)
            ple(0)

            def scaled(tile, dst, ready, n):
                pool.wait_ge(s.evacuated, count(tile + 1))
                pool.wait_ge(s.rstd_ready, count(4))
                pool.tensor_tensor(dst, sm[:, tile.slot(4), :], rstd[:], ALU.mult).then_inc(ready, 1)

            def decayed(hd, a, b):
                for k in range(a, b):
                    m = 1 << k
                    pool.wait_ge(s.ex_done, ahead(hd * 8 + k + 1))
                    if k == 0:
                        pool.wait_ge(s.k_ready, count(hd + 1))
                        pool.wait_ge(s.qg_ready, count(hd * 2 + 1))
                        pool.wait_ge(s.lvl_done, ahead(hd * len(GROUPS)))
                    pool.tensor_tensor(cl[:, k, :].rearrange("p (n g m) -> p n g m", g=2, m=m), ex[:, k % 2, :].rearrange("p (n g m) -> p n g m", g=2, m=m),
                                       pairs(kq, m), ALU.mult).then_inc(s.cl_ready, 1)

            def head(hd, units, mix):
                t0 = hd * 4 + TILE["h"]
                pv = hd - 1
                if mix:
                    decayed(pv, LEAD, 4)
                if units:
                    pool.wait_ge(s.sig_done, count(hd * 2))
                    scaled(t0, fqg[:, 0, :], s.z_ready, hd * 4)
                if mix:
                    decayed(pv, 4, 8)
                if units:
                    scaled(t0 + 1, fqg[:, 1, :], s.z_ready, hd * 4)
                    scaled(t0 + 2, fqg[:, 2, :], s.z_ready, hd * 4)
                    pool.wait_ge(s.z_ready, count(hd * 4 + 3))
                    pool.wait_ge(s.sig_done, count(hd * 2 + 1))
                    pool.wait_ge(s.cl_ready, ahead(hd * 8))
                    pool.wait_ge(s.diag_done, count(hd))
                    pool.tensor_tensor(kq[:, T:2 * T], fqg[:, 1, :], sg[:, 1, :], ALU.mult).then_inc(s.qg_ready, 1)
                    decayed(hd, 0, 1)
                    pool.wait_ge(s.hv_turned, count(hd))
                    scaled(t0 + 3, vtr[:], s.z_ready, hd * 4)
                    decayed(hd, 1, LEAD)
                    pool.wait_ge(s.o_step, ahead(hd * 2))
                    pool.tensor_tensor(gs[:], fqg[:, 2, :], sg[:, 2, :], ALU.mult).then_inc(s.qg_ready, 1)

            head(Lin(0), True, False)
            with pool.Fori(0, HEADS - 1) as i:
                head(Lin(1, 1, i), True, True)
            head(Lin(HEADS), False, True)

            out_proj(1)
            ffn(1)
            ple(1)

        @block.tensor
        def _(pe):
            for a in ahead_pe:
                pe.sem_inc(a, AHEAD)

            def unit(u, K, tile, rhs, need=None, blocks=range(16)):
                for b in blocks:
                    kt, t = b % K, b // K
                    if b % 8 == 0:
                        pe.wait_ge(s.lo_done, count(u * 2 + b // 8 + 1))
                    if kt == 0:
                        pe.wait_ge(s.evacuated, count(tile + (t - 3)))
                    if need is not None and t == 0:
                        pe.wait_ge(need[0], need[1] + kt + 1)
                    x = rhs(kt)
                    dst = bank[(tile + t).slot(4)]
                    w = slice(b * P, (b + 1) * P)
                    pe.matmul(dst[:, 0:2 * T], whi[:, u.slot(2), w], x, start=(kt == 0), stop=False, skip_group_check=True)
                    mm = pe.matmul(dst[:, 0:T], wlo[:, u.slot(2), w], x[:, 0:T], start=False, stop=(kt == K - 1), skip_group_check=True)
                    if b % 4 == 3:
                        mm.then_inc(s.quarter_done, 1)

            def norm_sum(nn):
                pe.wait_ge(s.sq_added, count(16 * nn + 16))
                pe.matmul(bank[4][:, 0:T], ones, sqacc[:], start=True, stop=True).then_inc(s.norm_summed, 1)

            def of(buf):
                return lambda kt: buf[:, kt, :]

            def turn_v(g):
                pe.wait_ge(s.evacuated, count(TILE["v"] + 4 * g + 4))
                pe.wait_ge(s.v_stored, count(2 * g))
                for t in range(2):
                    for k in range(4):
                        mm = pe.transpose(bank[4 + t][:, k * P:(k + 1) * P], vraw(4 * g + k)[:, t * P:(t + 1) * P], ident)
                mm.then_inc(s.v_turned, 1)

            def qk_sums(pr):
                pe.wait_ge(s.q_squared, count(pr * 3 + 3))
                pe.wait_ge(s.skpe_done, 1)
                for a in range(2):
                    pe.wait_ge(s.qk_log, ahead(pr * 2 + (a - 1)))
                    r = slice(64 * a, 64 * a + 64)
                    for w, (sq, pe_sq) in enumerate(((sqq, sqp), (sqk, skpe))):
                        pe.matmul(bank[6 + a][:, w * T:(w + 1) * T], ones, sq[:, a, :], start=True, stop=False, skip_group_check=True)
                        mm = pe.matmul(bank[6 + a][:, w * T:(w + 1) * T], ones[r, :], pe_sq[r, :], start=False, stop=True, skip_group_check=True)
                    mm.then_inc(s.qk_summed, 1)

            for j in range(U_A):
                unit(Lin(j), 16, Lin(j), of(xa), (s.x_ready, 0) if j == 0 else None)
                if j == 3:
                    pe.wait_ge(s.mat_in, 16)
                    norm_sum(0)
                if j == 5:
                    pe.wait_ge(s.cacc_done, count(4))
                    pe.matmul(bank[5][:, 0:T], ones, cacc[:, 0, :], start=True, stop=True).then_inc(s.c_summed, 1)
            tile = TILE["q"]
            for n, u in enumerate(range(BASE["q"], BASE["o0"])):
                if n < U_Q:
                    unit(Lin(u), 4, Lin(tile), of(xc), (s.xc_ready, 0) if n == 0 else None)
                else:
                    unit(Lin(u), 4, Lin(tile), lambda kt: xc[:, 4 + kt, :], (s.xc_ready, 4) if n == U_Q else None)
                tile += 4
                if n == 0:
                    pe.wait_ge(s.cacc_done, count(8))
                    pe.wait_ge(s.c_log, count(1))
                    pe.matmul(bank[5][:, T:2 * T], ones, cacc[:, 1, :], start=True, stop=True).then_inc(s.c_summed, 1)
                    pe.wait_ge(s.kg_ready, count(1))
                    pe.matmul(bank[6][:, 0:T], rot, kg[:], start=True, stop=True).then_inc(s.k_rotated, 1)
                g = n - (U_Q + U_K) - 1
                if g >= 0:
                    turn_v(g)
            qk_sums(Lin(0))
            turn_v(3)

            def q_turn(pr):
                pe.wait_ge(s.qk_scaled, ahead(pr * 6 + 2))
                pe.matmul(bank[2][:, 0:T], rot, qps[:], start=True, stop=True).then_inc(s.q_rotated, 1)

            def scores(pr):
                for a in range(2):
                    hd = pr * 2 + a
                    r = slice(64 * a, 64 * a + 64)
                    pe.wait_ge(s.q_roped, ahead(pr + 1))
                    pe.wait_ge(s.qk_scaled, ahead(pr * 6 + 6))
                    pe.wait_ge(s.masked, ahead(hd * 3 - 2))
                    for b in range(2):
                        cols = slice(P * b, P * b + P * (b + 1))
                        q0 = slice(P * b, P * b + P)
                        pe.matmul(bank[3 + a][:, cols], qs[:, a, q0], ks[:, a, 0:P * (b + 1)], start=True, stop=False, skip_group_check=True)
                        mm = pe.matmul(bank[3 + a][:, cols], qpr[r, q0], kps[r, 0:P * (b + 1)], start=False, stop=True, skip_group_check=True)
                    mm.then_inc(s.scored, 1)

            def turn_probs(pr, a):
                hd = pr * 2 + a
                pe.wait_ge(s.probs_ready, count(hd * 2 + 2))
                pe.wait_ge(s.pt_copied, ahead(hd - 1))
                pe.transpose(bank[a][:, 0:P], pb[:, a, 0, 0:P], ident)
                pe.transpose(bank[a][:, P:2 * P], pb[:, a, 1, 0:P], ident)
                pe.transpose(bank[a][:, 2 * P:3 * P], pb[:, a, 1, P:2 * P], ident).then_inc(s.turned, 1)

            def attend(pr, nxt, ahead_sums):
                if ahead_sums:
                    qk_sums(pr + 2)
                if nxt:
                    q_turn(pr + 1)
                turn_probs(pr, 0)
                turn_probs(pr, 1)
                for a in range(2):
                    hd = pr * 2 + a
                    pe.wait_ge(s.pt_copied, ahead(hd + 1))
                    pe.wait_ge(s.v_picked, count(pr + 1))
                    pe.wait_ge(s.ox_ready, ahead(pr * 2))
                    pe.matmul(bank[5][:, a * T:(a + 1) * T], vs[:, 0, a * P:(a + 1) * P], pts[:, a, 0:T], start=True, stop=False, skip_group_check=True)
                    pe.matmul(bank[5][:, a * T + P:(a + 1) * T], vs[:, 1, a * P:(a + 1) * P], pts[:, a, T:3 * P], start=False, stop=True,
                              skip_group_check=True).then_inc(s.o_done, 1)
                if nxt:
                    scores(pr + 1)

            q_turn(Lin(0))
            qk_sums(Lin(1))
            scores(Lin(0))
            with pe.Fori(0, PAIRS - 2) as i:
                attend(Lin(0, 1, i), True, True)
            attend(Lin(PAIRS - 2), True, False)
            attend(Lin(PAIRS - 1), False, False)

            def out_unit(layer, n, blocks=range(16)):
                need = (s.ox_ready, 16 * layer + AHEAD) if not n.moving and n.c == 0 else None
                unit(n + BASE[f"o{layer}"], 16, n + TILE[f"o{layer}"], of((xb, xa)[layer]), need, blocks)

            def out_proj(layer):
                for k in range(4):
                    out_unit(layer, Lin(k), range(15, 16) if layer == 1 and k == 0 else range(16))
                with pe.Fori(0, KT // 4 - 1) as i:
                    for k in range(4, 8):
                        out_unit(layer, Lin(k, 4, i))

            def ffn(layer):
                u0, t0 = BASE[f"f{layer}"], TILE[f"f{layer}"]
                x, nn = ((xa, 1), (xb, 4))[layer]
                for k in range(2 * CH):
                    unit(Lin(u0 + k), 16, Lin(t0 + k), of(x), (s.x_ready, 16 * nn) if k == 0 else None)
                    if k == 0:
                        norm_sum(nn)
                with pe.Fori(0, (NCH - 1) // 2) as i:
                    for cc in range(2):
                        for k in range(CH):
                            u = Lin(u0 + 8 + 12 * cc + 3 * k, 24, i)
                            t = Lin(t0 + 8 + 24 * cc + 6 * k, 48, i)
                            unit(u, 16, t, of(x))
                            unit(u + 1, 16, t + 1, of(x))
                            pe.wait_ge(s.hid_ready, count(Lin(FFT * layer + 4 + 4 * cc, 8, i)))
                            unit(u + 2, 4, t + 2, lambda kt, c=cc: hid[:, c, kt, :])
                for k in range(4):
                    pe.wait_ge(s.hid_ready, count(FFT * layer + FFT))
                    unit(Lin(u0 + 128 + k), 4, Lin(t0 + 248 + 4 * k), lambda kt: hid[:, 0, kt, :])

            def ple(layer):
                u0, t0 = BASE[f"pp{layer}"], TILE[f"pp{layer}"]
                pe.wait_ge(s.p_ready, count(layer + 1))
                for k in range(2):
                    unit(Lin(u0 + k), 2, Lin(t0 + 8 * k), lambda kt: pts2[:, kt, :])
                norm_sum((2, 5)[layer])
                u0, t0 = BASE[f"pg{layer}"], TILE[f"pg{layer}"]
                with pe.Fori(0, KT // 4) as i:
                    for k in range(4):
                        unit(Lin(u0 + k, 4, i), 16, Lin(t0 + k, 4, i), of((xa, xb)[layer]), (s.x_ready, (32, 80)[layer]) if k == 0 else None)

            out_proj(0)
            ffn(0)
            ple(0)

            def head(hd, units, mix):
                u0, t0 = hd * 4 + BASE["h"], hd * 4 + TILE["h"]
                pv = hd - 1
                first = (s.x_ready, 48) if not mix else None
                if not units:
                    out_unit(1, Lin(0), range(8))
                if units:
                    unit(u0, 16, t0, of(xb), first)
                    if not mix:
                        norm_sum(3)
                if mix:
                    pe.wait_ge(s.k_ready, count(pv + 1))
                    pe.wait_ge(s.qg_ready, count(pv * 2 + 1))
                    pe.wait_ge(s.am_step, ahead(pv * 9))
                    for t in range(2):
                        mm = pe.matmul(bank[5][:, t * P:(t + 1) * P], kq[:, t * P:(t + 1) * P], kq[:, T + t * P:T + (t + 1) * P], start=True, stop=True,
                                       skip_group_check=True)
                    mm.then_inc(s.diag_done, 1)
                    level_scores(pv, *GROUPS[0])
                if units:
                    unit(u0 + 1, 16, t0 + 1, of(xb))
                else:
                    out_unit(1, Lin(0), range(8, 12))
                if mix:
                    pe.wait_ge(s.z_ready, count(pv * 4 + 4))
                    pe.wait_ge(s.o_step, ahead(pv * 2))
                    pe.transpose(bank[4][:, 0:P], vtr[:, 0:P], ident)
                    pe.transpose(bank[4][:, P:2 * P], vtr[:, P:2 * P], ident).then_inc(s.hv_turned, 1)
                    level_scores(pv, *GROUPS[1])
                if units:
                    unit(u0 + 2, 16, t0 + 2, of(xb))
                else:
                    out_unit(1, Lin(0), range(12, 15))
                if mix:
                    level_scores(pv, *GROUPS[2])
                if units:
                    unit(u0 + 3, 16, t0 + 3, of(xb), None, range(8))
                if mix:
                    pe.wait_ge(s.am_step, ahead(pv * 9 + 9))
                    pe.wait_ge(s.hv_copied, count(pv + 1))
                    pe.wait_ge(s.o_step, ahead(pv * 2))
                    pe.matmul(bank[4][:, T:2 * T], vtok[:, 0, :], am[:, 0:2, :], start=True, stop=False, skip_group_check=True)
                    pe.matmul(bank[4][:, T + P:2 * T], vtok[:, 1, :], am[:, 2, :], start=False, stop=True, skip_group_check=True).then_inc(s.ho_done, 1)
                if units:
                    unit(u0 + 3, 16, t0 + 3, of(xb), None, range(8, 16))
                if mix:
                    pe.wait_ge(s.osq_done, count(pv + 1))
                    pe.matmul(bank[6][:, 0:T], ones, osq[:], start=True, stop=True).then_inc(s.o_summed, 1)

            def level_scores(pv, a, b):
                for k in range(a, b):
                    m = 1 << k
                    pe.wait_ge(s.cl_ready, ahead(pv * 8 + k + 1))
                    if k == 0:
                        pe.wait_ge(s.o_log, ahead(pv))
                    if k == LEVELS - 1:
                        pe.wait_ge(s.am_step, ahead(pv * 9 + 1))
                    if k == LEVELS:
                        mm = pe.matmul(bank[5][:, T:T + P], cl[:, k, 0:P], cl[:, k, P:T], start=True, stop=True, skip_group_check=True)
                    else:
                        bk, o = level_place(k)
                        for t in range(2):
                            half = cl[:, k, t * P:(t + 1) * P].rearrange("p (n g m) -> p n g m", g=2, m=m)[:, :, 1, :]
                            mm = pe.matmul(bank[bk][:, o + t * 64:o + (t + 1) * 64], cl[:, k, t * P:(t + 1) * P], half, start=True, stop=True,
                                           skip_group_check=True)
                mm.then_inc(s.lvl_done, 1)

            head(Lin(0), True, False)
            with pe.Fori(0, HEADS - 1) as i:
                head(Lin(1, 1, i), True, True)
            head(Lin(HEADS), False, True)

            out_proj(1)
            ffn(1)
            ple(1)


def _tiles(w, cols):
    k = w.shape[0] // P
    return w.reshape(k, P, w.shape[1])[:, :, cols].transpose(1, 0, 2)


def _full(w, cols):
    return _tiles(w, cols).reshape(P, UNIT)


def _many(w, groups):
    return np.concatenate([_tiles(w, g).reshape(P, -1) for g in groups], axis=1)


def _tile_cols(m):
    return np.arange(m * P, (m + 1) * P)


def _wstream(i):
    units = []
    w_a = i["mla_w_a"][0]
    pe_cols = np.arange(1024, 1088)
    for j in range(8):
        units.append(_full(w_a, _tile_cols(j)))
    units.append(_full(w_a, np.concatenate([pe_cols, pe_cols])))
    w_uq, w_ukv = i["mla_w_uq"][0], i["mla_w_ukv"][0]
    q = [np.arange(n * QK, n * QK + P) for n in range(HEADS)]
    q += [np.concatenate([np.arange(n * QK + P, (n + 1) * QK) for n in (2 * j, 2 * j + 1)]) for j in range(PAIRS)]
    k = [np.arange(n * 256, n * 256 + P) for n in range(HEADS)]
    v = [np.arange(n * 256 + P, n * 256 + 256) for n in range(HEADS)]
    for w, cols in ((w_uq, q), (w_ukv, k), (w_ukv, v)):
        units += [_many(w, cols[n:n + 4]) for n in range(0, len(cols), 4)]

    def ffn(layer):
        w_in, w_down = i["ffn_w_in"][layer], i["ffn_w_down"][layer]

        def pair(f):
            return [_full(w_in, _tile_cols(f)), _full(w_in, _tile_cols(FFT + f))]

        def down(chunk, j):
            rows = w_down[chunk * CH * P:(chunk + 1) * CH * P]
            return _many(rows, [_tile_cols(4 * j + t) for t in range(4)])

        for f in range(CH):
            units.extend(pair(f))
        for chunk in range(1, NCH):
            for j in range(CH):
                units.extend(pair(chunk * CH + j))
                units.append(down(chunk - 1, j))
        for j in range(CH):
            units.append(down(NCH - 1, j))
        for j in range(2):
            units.append(_many(i["ple_w_proj"][layer], [_tile_cols(8 * j + t) for t in range(8)]))
        for m in range(KT):
            units.append(_full(i["ple_w_gate"][layer], _tile_cols(m)))

    units += [_full(i["mla_w_o"][0], _tile_cols(m)) for m in range(KT)]
    ffn(0)
    w_in = i["hgrn_w_in"][0]
    for n in range(HEADS):
        for part in (1, 0, 3, 2):
            units.append(_full(w_in, _tile_cols(part * HEADS + n)))
    units += [_full(i["hgrn_w_o"][0], _tile_cols(m)) for m in range(KT)]
    ffn(1)
    assert len(units) == UNITS
    return np.stack(units)


def _table(i):
    def cols(a):
        return a.reshape(-1, P).T

    pe = QK - ROPE
    parts = [cols(i["mix_norm"]), cols(i["ffn_norm"]), cols(i["ple_norm"]), cols(i["mla_q_norm"]), cols(i["mla_kv_norm"])]
    for g in (i["mla_qk_gain_q"][0], i["mla_qk_gain_k"][0]):
        parts += [g[:pe, None], np.concatenate([g[pe:], g[pe:]])[:, None]]
    parts += [cols(i["hgrn_o_norm"]), cols(i["hgrn_lb_logits"]), cols(i["ffn_conv_w"]), cols(i["ffn_conv_b"])]
    freq = (10000.0 ** (-np.arange(0, ROPE, 2, dtype=np.float32) / np.float32(ROPE))).astype(np.float32)
    parts.append(np.tile(freq, 4)[:, None])
    return np.ascontiguousarray(np.concatenate(parts, axis=1))


def _matrices():
    m = np.zeros((P, 4, P), np.float32)
    m[:, 0] = 1.0
    m[:, 1] = np.eye(P)
    for b in (0, ROPE):
        for r in range(ROPE // 2):
            m[b + r + ROPE // 2, 2, b + r] = -1.0
            m[b + r, 2, b + r + ROPE // 2] = 1.0
    m[:, 3] = np.where(np.arange(P)[None, :] > np.arange(P)[:, None], np.float32(NEG), np.float32(0))
    return m


def _level_masks():
    out = []
    s = np.arange(P)[:, None]
    for k in range(LEVELS):
        m = 1 << k
        n = (np.arange(P // 2) // m)[None, :]
        keep = (s >= n * 2 * m) & (s < n * 2 * m + m)
        out += [keep, keep]
    out += [np.eye(P, dtype=bool)] * 2
    return np.concatenate(out, axis=1).astype(np.int32)


def kernel(**inputs):
    import concourse.bacc as _bacc
    from concourse.bass_utils import run_bass_kernel_spmd as _run

    i = {k: np.asarray(v) for k, v in inputs.items()}
    arrays = {
        "wstream": _wstream(i),
        "x_t": np.ascontiguousarray(i["x"][0].T),
        "p_t": np.ascontiguousarray(i["p"][:, 0].transpose(0, 2, 1)),
        "positions": np.ascontiguousarray(i["positions"]),
        "table": _table(i),
        "matrices": _matrices(),
        "level_masks": _level_masks(),
    }
    nc = _bacc.Bacc("TRN2", target_bir_lowering=False, num_devices=1)
    args = [nc.dram_tensor(name, a.shape, mybir.dt.from_np(a.dtype), kind="ExternalInput").ap() for name, a in arrays.items()]
    args.append(nc.dram_tensor("out_t", (D, T), F32, kind="ExternalOutput").ap())
    build(nc, *args)
    r = _run(nc, [arrays], core_ids=[0])
    return np.ascontiguousarray(np.asarray(r.results[0]["out_t"]).T)[None]
```
